# Optimizing a Trainium2 kernel written in Bass

```python
import jax, jax.numpy as jnp
from jax import lax
import numpy as np

D_MODEL = 2048
BATCH = 1
SEQ = 512
DEPTH = 1

CHUNK = 64
Q_BLOCK = 128
MIX_WIDTH = D_MODEL

RWKV_HEAD_DIM = 64
RWKV_WIDTH = MIX_WIDTH // 2
RWKV_HEADS = RWKV_WIDTH // RWKV_HEAD_DIM
DECAY_LORA = 96
ICLR_LORA = 96
GATE_LORA = 256
GN_EPS = 64e-5

QK_NOPE_DIM = 128
QK_ROPE_DIM = 64
V_HEAD_DIM = 128
MLA_WIDTH = MIX_WIDTH - RWKV_WIDTH
MLA_HEADS = MLA_WIDTH // V_HEAD_DIM
Q_LORA_RANK = 512
KV_LORA_RANK = 256
ROPE_THETA = 10000.0

D_FF = 5632
CONV_WIDTH = 3

NORM_EPS = 1e-6
N_MOD = 6

RWKV_COLS = 3 * RWKV_WIDTH + DECAY_LORA + ICLR_LORA + GATE_LORA
MLA_COLS = Q_LORA_RANK + KV_LORA_RANK + QK_ROPE_DIM
IN_COLS = RWKV_COLS + MLA_COLS

kernel_name = "hybrid_rwkv7_mla_convffn_block"

def rms_norm(x, g):
    xf = x.astype(jnp.float32)
    y = xf * lax.rsqrt(jnp.mean(xf * xf, axis=-1, keepdims=True) + NORM_EPS)
    return (y * g.astype(jnp.float32)).astype(x.dtype)

def shift_prev(u):
    return jnp.pad(u, ((0, 0), (1, 0), (0, 0)))[:, :-1]

def apply_rope(u, cos, sin):
    u1, u2 = jnp.split(u, 2, axis=-1)
    return jnp.concatenate([u1 * cos - u2 * sin, u1 * sin + u2 * cos], axis=-1)

def rwkv7_mixer(p, mu_shift, w0, w_decay_up, a0, w_iclr_up, w_gate_up, k_k, k_a, r_k, ln_x_g, ln_x_b):
    B, S, _ = p.shape
    H, N, W = RWKV_HEADS, RWKV_HEAD_DIM, RWKV_WIDTH
    f32 = jnp.float32
    p = p + (shift_prev(p) - p) * mu_shift
    r, k, v, wd, ad, gd = jnp.split(
        p, [W, 2 * W, 3 * W, 3 * W + DECAY_LORA, 3 * W + DECAY_LORA + ICLR_LORA], axis=-1)
    w_log = -jax.nn.softplus(-(w0 + jnp.tanh(wd) @ w_decay_up)) - 0.5
    decay = jnp.exp(-jnp.exp(w_log.astype(f32)))
    a = jax.nn.sigmoid(a0 + ad @ w_iclr_up)
    g = jax.nn.sigmoid(gd) @ w_gate_up
    kk = (k * k_k).reshape(B, S, H, N).astype(f32)
    kk = kk / jnp.maximum(jnp.sqrt(jnp.sum(kk * kk, axis=-1, keepdims=True)), 1e-12)
    k = k * (1.0 + (a - 1.0) * k_a)

    def heads(t):
        return t.reshape(B, S, H, N).astype(f32)

    r_h, k_h, v_h, w_h, a_h = heads(r), heads(k), heads(v), heads(decay), heads(a)

    def step(state, inp):
        r_t, w_t, k_t, v_t, kk_t, a_t = inp
        sa = jnp.einsum('bhvk,bhk->bhv', state, -kk_t)
        state = (state * w_t[:, :, None, :]
                 + sa[..., None] * (kk_t * a_t)[:, :, None, :]
                 + v_t[..., None] * k_t[:, :, None, :])
        y_t = jnp.einsum('bhvk,bhk->bhv', state, r_t)
        return state, y_t

    xs = tuple(jnp.moveaxis(t, 1, 0) for t in (r_h, w_h, k_h, v_h, kk, a_h))
    _, y = lax.scan(step, jnp.zeros((B, H, N, N), f32), xs)
    y = jnp.moveaxis(y, 0, 1)
    mean = jnp.mean(y, axis=-1, keepdims=True)
    var = jnp.mean(jnp.square(y - mean), axis=-1, keepdims=True)
    y = ((y - mean) * lax.rsqrt(var + GN_EPS)).reshape(B, S, W) * ln_x_g + ln_x_b
    bonus = jnp.sum(r_h * k_h * r_k, axis=-1, keepdims=True) * v_h
    y = (y + bonus.reshape(B, S, W)) * g
    return y.astype(p.dtype)

def mla_mixer(p, positions, q_norm_g, w_q_up, kv_norm_g, w_kv_up):
    B, S, _ = p.shape
    H, DN, DR, DV = MLA_HEADS, QK_NOPE_DIM, QK_ROPE_DIM, V_HEAD_DIM
    f32 = jnp.float32
    q_lat, kv_lat, k_rope = jnp.split(p, [Q_LORA_RANK, Q_LORA_RANK + KV_LORA_RANK], axis=-1)
    q = (rms_norm(q_lat, q_norm_g) @ w_q_up).reshape(B, S, H, DN + DR)
    q_nope, q_rope = q[..., :DN], q[..., DN:]
    kv = (rms_norm(kv_lat, kv_norm_g) @ w_kv_up).reshape(B, S, H, DN + DV)
    k_nope, v = kv[..., :DN], kv[..., DN:]
    inv_freq = ROPE_THETA ** (-jnp.arange(0, DR, 2, dtype=f32) / DR)
    ang = positions.astype(f32)[..., None] * inv_freq
    cos, sin = jnp.cos(ang), jnp.sin(ang)
    q_rope = apply_rope(q_rope.astype(f32), cos[:, :, None], sin[:, :, None]).astype(q.dtype)
    k_rope = apply_rope(k_rope.astype(f32), cos, sin).astype(q.dtype)
    scale = (DN + DR) ** -0.5
    n_blk = S // Q_BLOCK
    k_chunk = jnp.arange(S) // CHUNK

    def q_block(args):
        i, qn, qr = args
        s = (jnp.einsum('bqhd,bkhd->bhqk', qn, k_nope)
             + jnp.einsum('bqhr,bkr->bhqk', qr, k_rope)).astype(f32) * scale
        q_chunk = (i * Q_BLOCK + jnp.arange(Q_BLOCK)) // CHUNK
        mask = q_chunk[:, None] >= k_chunk[None, :]
        s = jnp.where(mask[None, None], s, -jnp.inf)
        prob = jax.nn.softmax(s, axis=-1).astype(v.dtype)
        return jnp.einsum('bhqk,bkhd->bqhd', prob, v)

    qn_b = q_nope.reshape(B, n_blk, Q_BLOCK, H, DN).transpose(1, 0, 2, 3, 4)
    qr_b = q_rope.reshape(B, n_blk, Q_BLOCK, H, DR).transpose(1, 0, 2, 3, 4)
    o = lax.map(q_block, (jnp.arange(n_blk), qn_b, qr_b))
    return o.transpose(1, 0, 2, 3, 4).reshape(B, S, H * DV)

def conv_ffn(h, w_ffn_up, conv_w, conv_b, w_ffn_down):
    S = h.shape[1]
    u = h @ w_ffn_up
    up = jnp.pad(u, ((0, 0), (CONV_WIDTH - 1, 0), (0, 0)))
    uc = conv_b + conv_w[CONV_WIDTH - 1] * u
    for j in range(CONV_WIDTH - 1):
        uc = uc + conv_w[j] * up[:, j:j + S]
    gate, val = jnp.split(uc, 2, axis=-1)
    return (jax.nn.gelu(gate, approximate=True) * val) @ w_ffn_down

def setup_inputs(seed: int = 0) -> dict:
    key = jax.random.key(seed)
    ks = iter(jax.random.split(key, 40))
    L, D = DEPTH, D_MODEL
    f32 = jnp.float32

    def nrm(shape, scale):
        return jax.random.normal(next(ks), shape, f32) * scale

    def gain(shape):
        return 1.0 + nrm(shape, 0.02)

    x = nrm((BATCH, SEQ, D), 1.0)
    c = nrm((BATCH, D), 1.0)
    start = jax.random.randint(next(ks), (BATCH, 1), 0, 8192, dtype=jnp.int32)
    positions = (start + jnp.arange(SEQ, dtype=jnp.int32)[None, :]).astype(jnp.int32)
    return {
        "x": x,
        "c": c,
        "positions": positions,
        "w_mod": nrm((L, D, N_MOD * D), D ** -0.5),
        "b_mod": nrm((L, N_MOD * D), 0.01),
        "g_pre_mix": gain((L, D)),
        "w_in": nrm((L, D, IN_COLS), D ** -0.5),
        "mu_shift": jax.random.uniform(next(ks), (L, RWKV_COLS), f32),
        "w0": jax.random.uniform(next(ks), (L, RWKV_WIDTH), f32, -6.0, 1.0),
        "w_decay_up": nrm((L, DECAY_LORA, RWKV_WIDTH), 0.1 * DECAY_LORA ** -0.5),
        "a0": nrm((L, RWKV_WIDTH), 0.1),
        "w_iclr_up": nrm((L, ICLR_LORA, RWKV_WIDTH), 0.5 * ICLR_LORA ** -0.5),
        "w_gate_up": nrm((L, GATE_LORA, RWKV_WIDTH), GATE_LORA ** -0.5),
        "k_k": 0.85 + nrm((L, RWKV_WIDTH), 0.02),
        "k_a": gain((L, RWKV_WIDTH)),
        "r_k": nrm((L, RWKV_HEADS, RWKV_HEAD_DIM), 0.1),
        "ln_x_g": gain((L, RWKV_WIDTH)),
        "ln_x_b": nrm((L, RWKV_WIDTH), 0.01),
        "q_norm_g": gain((L, Q_LORA_RANK)),
        "w_q_up": nrm((L, Q_LORA_RANK, MLA_HEADS * (QK_NOPE_DIM + QK_ROPE_DIM)), Q_LORA_RANK ** -0.5),
        "kv_norm_g": gain((L, KV_LORA_RANK)),
        "w_kv_up": nrm((L, KV_LORA_RANK, MLA_HEADS * (QK_NOPE_DIM + V_HEAD_DIM)), KV_LORA_RANK ** -0.5),
        "w_out": nrm((L, MIX_WIDTH, D), MIX_WIDTH ** -0.5),
        "g_post_mix": gain((L, D)),
        "g_pre_ffn": gain((L, D)),
        "w_ffn_up": nrm((L, D, 2 * D_FF), D ** -0.5),
        "conv_w": nrm((L, CONV_WIDTH, 2 * D_FF), CONV_WIDTH ** -0.5),
        "conv_b": nrm((L, 2 * D_FF), 0.01),
        "w_ffn_down": nrm((L, D_FF, D), D_FF ** -0.5),
        "g_post_ffn": gain((L, D)),
    }

def reference(x, c, positions, w_mod, b_mod, g_pre_mix, w_in, mu_shift, w0, w_decay_up, a0,
              w_iclr_up, w_gate_up, k_k, k_a, r_k, ln_x_g, ln_x_b, q_norm_g, w_q_up, kv_norm_g,
              w_kv_up, w_out, g_post_mix, g_pre_ffn, w_ffn_up, conv_w, conv_b, w_ffn_down, g_post_ffn):
    silu_c = jax.nn.silu(c)
    for l in range(DEPTH):
        mod = (silu_c @ w_mod[l] + b_mod[l])[:, None, :]
        shift_m, scale_m, gate_m, shift_f, scale_f, gate_f = jnp.split(mod, N_MOD, axis=-1)

        h = rms_norm(x, g_pre_mix[l]) * (1.0 + scale_m) + shift_m
        p = h @ w_in[l]
        y_rwkv = rwkv7_mixer(p[..., :RWKV_COLS], mu_shift[l], w0[l], w_decay_up[l], a0[l],
                             w_iclr_up[l], w_gate_up[l], k_k[l], k_a[l], r_k[l],
                             ln_x_g[l], ln_x_b[l])
        y_mla = mla_mixer(p[..., RWKV_COLS:], positions, q_norm_g[l], w_q_up[l],
                          kv_norm_g[l], w_kv_up[l])
        o = jnp.concatenate([y_rwkv, y_mla], axis=-1) @ w_out[l]
        x = x + gate_m * rms_norm(o, g_post_mix[l])

        h = rms_norm(x, g_pre_ffn[l]) * (1.0 + scale_f) + shift_f
        o = conv_ffn(h, w_ffn_up[l], conv_w[l], conv_b[l], w_ffn_down[l])
        x = x + gate_f * rms_norm(o, g_post_ffn[l])
    return x


_drawn_inputs = setup_inputs


def setup_inputs(seed=0):
    import zlib

    import numpy as np

    out = dict(_drawn_inputs(seed))
    spreads = {}
    factors = {'b_mod': 3.207,
     'g_pre_mix': 3.853,
     'w_decay_up': 8.0,
     'a0': 3.214,
     'ln_x_g': 60.528,
     'ln_x_b': 200.0,
     'q_norm_g': 8.0,
     'kv_norm_g': 7.742,
     'g_post_mix': 5.339,
     'g_pre_ffn': 13.648,
     'conv_b': 31.053,
     'g_post_ffn': 66.433,
     'k_k': 21.391}
    for name, (base, spread) in spreads.items():
        noise = np.random.default_rng([zlib.crc32(name.encode()), seed]).standard_normal(out[name].shape)
        drawn = base * np.exp(spread * noise) if base else spread * noise
        out[name] = __import__('jax').numpy.asarray(drawn.astype(out[name].dtype))
    for name, factor in factors.items():
        out[name] = (out[name] * factor).astype(out[name].dtype)
    return out
```

```python
import math
from contextlib import ExitStack

import concourse.bass as bass
from concourse import mybir
import numpy as np

F32 = mybir.dt.float32
F32R = mybir.dt.float32r
I32 = mybir.dt.int32
ALU = mybir.AluOpType
ACT = mybir.ActivationFunctionType
AX_X = mybir.AxisListType.X

P = 128
D = 2048
T = 512
KD = D // P
CH = 64
NCH = T // CH
NPAIR = 8
LATQ, LATKV = 4, 2
NOPE, ROPE = 128, 64
SCALE = float(NOPE + ROPE) ** -0.5
FF = 5632
FT = FF // P
GROUPS = 4
GT = FT // GROUPS
UNIT = 8 * P
DUNIT = GT * P
NMOD = 6 * D // P
GRP = 1024
EPS = 1e-6
GN_EPS = 64e-5
DECAY_C = math.exp(-0.5)
LEVELS = [2, 4, 8, 16, 32]

VEC = {}
_at = 0
for _n, _w in (("c", 16), ("b_mod", 96), ("g_pre_mix", 16), ("g_post_mix", 16), ("g_pre_ffn", 16),
               ("g_post_ffn", 16), ("mu", 28), ("w0", 8), ("a0", 8), ("k_k", 8), ("k_a", 8),
               ("r_k", 8), ("ln_g", 8), ("ln_b", 8), ("q_g", 4), ("kv_g", 2), ("conv", 8 * FT)):
    VEC[_n] = _at
    _at += _w
NVEC = _at

CON = {}
_at = 0
for _n, _w in (("ident", P), ("ones", P), ("heads", P), ("below", CH), ("upto", CH), ("m1t", P), ("m1", P),
               ("m2", P), ("m4", P), ("m8", P), ("m16", P), ("m32", P), ("swap", P), ("early", P), ("late", P),
               ("reset", T), ("freq", 1)):
    CON[_n] = _at
    _at += _w
NCON = _at


def constants():
    con = np.zeros((P, NCON), np.float32)

    def put(name, a):
        con[:, CON[name]:CON[name] + a.shape[1]] = a

    i = np.arange(P)
    head = i[:, None] // CH == i[None, :] // CH
    put("ident", np.eye(P))
    put("ones", np.ones((P, P)))
    put("heads", head)
    j, t = (i % CH)[:, None], np.arange(CH)[None, :]
    put("below", j < t)
    put("upto", j <= t)
    for b in (1, 2, 4, 8, 16, 32):
        row, col = i[:, None], i[None, :]
        m = (row // (2 * b) == col // (2 * b)) & (row % (2 * b) >= b) & (col % (2 * b) < b)
        put(f"m{b}", m)
        if b == 1:
            put("m1t", m.T)
    swap = np.zeros((P, P))
    for m in range(P):
        h, r = m // ROPE * ROPE, m % ROPE
        if r < ROPE // 2:
            swap[h + r + ROPE // 2, m] = -1.0
        else:
            swap[h + r - ROPE // 2, m] = 1.0
    put("swap", swap)
    early = np.zeros((P, P))
    early[0, :CH] = 1.0
    late = np.zeros((P, P))
    late[0, CH:] = -1e30
    put("early", early)
    put("late", late)
    reset = np.ones((P, T))
    reset[:, ::CH] = 0.0
    put("reset", reset)
    freq = 10000.0 ** (-np.arange(0, ROPE, 2) / ROPE)
    put("freq", np.tile(freq.astype(np.float32), P // (ROPE // 2))[:, None])
    return con


class Mem:

    def __init__(self, nc):
        self.nc = nc
        at = (nc.sbuf_base + 63) // 64 * 64
        self.h = at
        self.z = self.h + 2 * KD * T * 4
        self.con = self.z + KD * T * 4
        self.ring = self.con + (NCON + NVEC + NMOD + 4 * KD + 28 + 8 + KD) * 4 + 7 * 64
        self.ring = (self.ring + 63) // 64 * 64
        self.work = self.ring + 6 * UNIT * 4
        self.end = nc.sbuf_usable_end
        self.whole = None

    def put(self, name, shape, dtype, offset):
        size = 4
        for n in shape[1:]:
            size *= n
        assert offset + size <= self.end, (name, offset + size - self.end)
        if dtype == F32 and offset >= self.work:
            if self.whole is None:
                self.whole = self.nc.alloc_sbuf_tensor_at("work", [P, (self.end - self.work) // 4], F32,
                                                          offset=self.work)
            start = (offset - self.work) // 4
            view = self.whole[:, start:start + size // 4]
            if len(shape) == 3:
                view = view.rearrange("p (a n) -> p a n", n=shape[2])
            if len(shape) == 4:
                view = view.rearrange("p (a b n) -> p a b n", b=shape[2], n=shape[3])
            return view, (offset + size + 63) // 64 * 64
        return self.nc.alloc_sbuf_tensor_at(name, shape, dtype, offset=offset), (offset + size + 63) // 64 * 64


def build_program(nc, d, out):
    with ExitStack() as ctx:
        mem = Mem(nc)
        m = {}
        m["h_hi"], at = mem.put("h_hi", [P, KD, T], F32R, mem.h)
        m["h_lo"], at = mem.put("h_lo", [P, KD, T], F32R, at)
        put_ring(mem, m, "w", UNIT)
        m["z"], at = mem.put("z", [P, KD, T], F32, mem.z)
        m["con"], at = mem.put("con", [P, NCON], F32, mem.con)
        m["vec"], at = mem.put("vec", [P, NVEC], F32, at)
        m["mod"], at = mem.put("mod", [P, NMOD], F32, at)
        m["gs"], at = mem.put("gs", [P, 4 * KD], F32, at)
        m["omm"], at = mem.put("omm", [P, 28], F32, at)
        m["eps"], at = mem.put("eps", [P, 8], F32, at)
        m["silu"], at = mem.put("silu", [P, KD], F32, at)
        m["bank"] = [ctx.enter_context(nc.psum_tensor(f"bank{b}", [P, T], F32)) for b in range(8)]
        stage_modulation(nc, mem, m, d)
        stage_normed_input(nc, mem, m, "mix", 0, 0)
        stage_rwkv(nc, mem, m, d)
        stage_latents(nc, mem, m, d)
        stage_attention(nc, mem, m, d)
        stage_mix_out(nc, mem, m, d)
        stage_normed_input(nc, mem, m, "ffn", 1, 3)
        stage_ffn(nc, mem, m, d, out)


def put_ring(mem, m, name, width):
    m["w_raw"], at = mem.put(name + "_raw", [P, 2, width], F32, mem.ring)
    m["w_hi"], at = mem.put(name + "_hi", [P, 2, width], F32R, at)
    m["w_lo"], at = mem.put(name + "_lo", [P, 2, width], F32R, at)
    return at


def con(m, name, n=None):
    at = CON[name]
    return m["con"][:, at:at + (n or P)]


def vec(m, name, i=0):
    return m["vec"][:, bass.ds(i + VEC[name], 1)]


def row(ap, i, axis=0):
    if axis == 0:
        return ap[bass.ds(i, 1)].rearrange("a p n -> p (a n)")
    return ap[:, bass.ds(i, 1), :].rearrange("p a n -> p (a n)")


def over(ap, n):
    w = ap.shape[1]
    return ap.rearrange("p (a w) -> p a w", a=1).broadcast_to([ap.shape[0], n, w])



def ring_sems(nc, ctx, stage):
    s = {f"raw_loaded{j}": nc.alloc_semaphore(f"{stage}_raw_loaded{j}") for j in range(2)}
    for n in ("hi_ready", "lo_ready", "unit_used"):
        s[n] = nc.alloc_semaphore(f"{stage}_{n}")
    return s


def load_unit(sp, m, s, u, slot, nth, src, width):
    sp.wait_ge(s["lo_ready"], u + 1)
    sp.dma_start(m["w_raw"][:, slot, 0:width], src).then_inc(s[f"raw_loaded{slot}"], 16)


def round_unit(act, m, s, u, slot, nth, width):
    act.wait_ge(s[f"raw_loaded{slot}"], (nth + 1) * 16)
    act.wait_ge(s["unit_used"], u + 1)
    act.activation(m["w_hi"][:, slot, 0:width], m["w_raw"][:, slot, 0:width], ACT.Copy).then_inc(s["hi_ready"], 1)


def remainder_unit(pool, m, s, u, slot, width):
    pool.wait_ge(s["hi_ready"], u + 1)
    pool.tensor_tensor(m["w_lo"][:, slot, 0:width], m["w_raw"][:, slot, 0:width],
                       m["w_hi"][:, slot, 0:width].bitcast(F32), ALU.subtract).then_inc(s["lo_ready"], 1)


def tile_done(eng, s, u):
    eng.wait_ge(s["unit_used"], u + 3)


def multiply_unit(pe, m, s, u, slot, bank, x_hi, x_lo, k0, n, first, last):
    multiply_part(pe, m, s, u, slot, bank, x_hi, x_lo, k0, 0, n, n, first, last)


def multiply_part(pe, m, s, u, slot, bank, x_hi, x_lo, k0, at, count, n, first, last):
    if at == 0:
        pe.wait_ge(s["lo_ready"], u + 3)
    for k in range(at, at + count):
        hi = m["w_hi"][:, slot, k * P:(k + 1) * P]
        lo = m["w_lo"][:, slot, k * P:(k + 1) * P]
        pe.matmul(bank, hi, x_hi[:, k0 + k, :], start=first and k == 0, stop=False)
        pe.matmul(bank, hi, x_lo[:, k0 + k, :], start=False, stop=False)
        mm = pe.matmul(bank, lo, x_hi[:, k0 + k, :], start=False, stop=last and k == n - 1)
    if at + count == n:
        mm.then_inc(s["unit_used"], 1)



def mod_sems(nc, stage, slots):
    s = {f"mod_landed{j}": nc.alloc_semaphore(f"{stage}_mod_landed{j}") for j in range(slots)}
    for n in ("mod_summed", "mod_cols", "mod_added"):
        s[n] = nc.alloc_semaphore(f"{stage}_{n}")
    return s


def load_mod(sp, s, buf, u, slot, src):
    sp.wait_ge(s["mod_summed"], u + 1)
    sp.dma_start(buf[:, slot, :], src).then_inc(s[f"mod_landed{slot}"], 16)


def add_mod(dve, m, s, buf, acc, u, slot, nth, slots, k, first=False):
    dve.wait_ge(s[f"mod_landed{slot}"], nth * 16 + 16)
    dve.wait_ge(s["mod_summed"], u + slots)
    column = m["silu"][:, bass.ds(k, 1)]
    if first:
        op = dve.tensor_scalar(acc, buf[:, slot, :], column, None, ALU.mult)
    else:
        op = dve.scalar_tensor_tensor(out=acc, in0=buf[:, slot, :], scalar=column, in1=acc, op0=ALU.mult, op1=ALU.add)
    op.then_inc(s["mod_summed"], 1)


def mod_columns(pe, m, s, bank, acc, c0, units):
    pe.wait_ge(s["mod_summed"], units)
    for q in range(acc.shape[1] // P):
        mm = pe.matmul(bank[:, c0 + q:c0 + q + 1], acc[:, q * P:(q + 1) * P], con(m, "ones", 1), start=True, stop=True)
    mm.then_inc(s["mod_cols"], 1)


def finish_mod(dve, m, s, bank, c0, n, groups, gain=None):
    dve.wait_ge(s["mod_cols"], groups + 2)
    dve.tensor_tensor(m["mod"][:, c0:c0 + n], bank[:, c0:c0 + n], m["vec"][:, VEC["b_mod"] + c0:VEC["b_mod"] + c0 + n],
                      ALU.add).then_inc(s["mod_added"], 1)
    which, g, col = gain
    dve.wait_ge(s["mod_added"], 1)
    dve.scalar_tensor_tensor(out=m["gs"][:, which * KD:(which + 1) * KD], in0=m["mod"][:, col:col + KD],
                             scalar=1.0 if which < 2 else 0.0, in1=m["vec"][:, VEC[g]:VEC[g] + KD],
                             op0=ALU.add, op1=ALU.mult).then_inc(s["mod_added"], 1)


def mod_unit(d, u):
    return row(d["w_mod"], u)


def stage_modulation(nc, mem, m, d):
    NB = 8
    GROUPS_HERE = 4
    with nc.cleanup_on_exit(), ExitStack() as ctx:
        s = {n: nc.alloc_semaphore("mod_" + n) for n in ("loads", "silu")}
        s.update(mod_sems(nc, "mod", NB))
        buf, at = mem.put("mod_buf", [P, NB, GRP], F32, mem.work)
        acc, at = mem.put("mod_acc", [P, 2, GRP], F32, at)
        sil = m["silu"]
        bank = m["bank"][0]
        blk = ctx.enter_context(nc.Block())

        @blk.sync
        def _(sp):
            sp.dma_start(m["vec"][:], d["vec"]).then_inc(s["loads"], 16)
            sp.dma_start(m["con"][:], d["con"]).then_inc(s["loads"], 16)
            with sp.Fori(0, GROUPS_HERE // 2) as i:
                for j in range(2 * KD):
                    load_mod(sp, s, buf, i * (2 * KD) + j, j % NB, mod_unit(d, i * (2 * KD) + j))
            sp.dma_start(m["z"][:], d["xt"]).then_inc(s["loads"], 16)
            sp.wait_ge(s["loads"], 48)

        @blk.scalar
        def _(act):
            act.wait_ge(s["loads"], 32)
            act.activation(sil[:], m["vec"][:, VEC["c"]:VEC["c"] + KD], ACT.Sigmoid).then_inc(s["silu"], 1)

        @blk.vector
        def _(dve):
            dve.sem_inc(s["mod_summed"], NB)
            dve.sem_inc(s["mod_cols"], 2)
            dve.wait_ge(s["silu"], 1)
            dve.tensor_tensor(sil[:], sil[:], m["vec"][:, VEC["c"]:VEC["c"] + KD], ALU.mult).then_inc(s["silu"], 1)
            dve.wait_ge(s["silu"], 2)
            dve.tensor_scalar(m["omm"][:], m["vec"][:, VEC["mu"]:VEC["mu"] + 28], -1.0, 1.0, ALU.mult, ALU.add)
            dve.memset(m["eps"][:, 0:1], EPS)
            dve.memset(m["eps"][:, 1:2], GN_EPS)
            dve.memset(m["eps"][:, 2:3], math.pi / 2)
            with dve.Fori(0, GROUPS_HERE // 2) as i:
                for j in range(2 * KD):
                    g, k = j // KD, j % KD
                    if k == 0:
                        dve.wait_ge(s["mod_cols"], i * 2 + (g + 1))
                    add_mod(dve, m, s, buf, acc[:, g, :], i * (2 * KD) + j, j % NB, i * (2 * KD // NB) + j // NB, NB,
                            k, k == 0)
            finish_mod(dve, m, s, bank, 0, 2 * KD, GROUPS_HERE, (0, "g_pre_mix", KD))

        @blk.tensor
        def _(pe):
            pe.wait_ge(s["loads"], 32)
            for g in range(GROUPS_HERE):
                mod_columns(pe, m, s, bank, acc[:, g % 2, :], g * (GRP // P), KD * (g + 1) + NB)


def stage_normed_input(nc, mem, m, stage, half, first_mod):
    with nc.cleanup_on_exit(), ExitStack() as ctx:
        def sem(n):
            return nc.alloc_semaphore(f"{stage}_{n}")
        squared, summed, root, rstd_ready = sem("squared"), sem("summed"), sem("root"), sem("rstd_ready")
        scaled, shifted, hi_ready, lo_ready = sem("scaled"), sem("shifted"), sem("hi_ready"), sem("lo_ready")
        sq, at = mem.put(f"{stage}_sq", [P, 2, T], F32, mem.work)
        rstd, at = mem.put(f"{stage}_rstd", [P, T], F32, at)
        tmp, at = mem.put(f"{stage}_tmp", [P, 4, T], F32, at)
        bank = m["bank"][0]
        z = m["z"]
        blk = ctx.enter_context(nc.Block())

        @blk.scalar
        def _(act):
            for k in range(KD):
                if k >= 2:
                    act.wait_ge(summed, k - 1)
                act.activation(sq[:, k % 2, :], z[:, k, :], ACT.Square).then_inc(squared, 1)
            act.wait_ge(summed, KD)
            act.activation(rstd[:], bank[:], ACT.Sqrt, bias=m["eps"][:, 0:1], scale=1.0 / D).then_inc(root, 1)
            for k in range(KD):
                act.wait_ge(shifted, k + 1)
                act.activation(m["h_hi"][:, k, :], tmp[:, k % 4, :], ACT.Copy).then_inc(hi_ready, 1)

        @blk.tensor
        def _(pe):
            for k in range(KD):
                pe.wait_ge(squared, k + 1)
                pe.matmul(bank[:], con(m, "ones"), sq[:, k % 2, :], start=k == 0, stop=k == KD - 1).then_inc(summed, 1)

        @blk.vector
        def _(dve):
            dve.wait_ge(root, 1)
            dve.reciprocal(rstd[:], rstd[:]).then_inc(rstd_ready, 1)
            dve.wait_ge(rstd_ready, 1)
            for k in range(KD):
                if k >= 4:
                    dve.wait_ge(lo_ready, k - 3)
                dve.scalar_tensor_tensor(out=tmp[:, k % 4, :], in0=z[:, k, :],
                                         scalar=m["gs"][:, half * KD + k:half * KD + k + 1], in1=rstd[:],
                                         op0=ALU.mult, op1=ALU.mult).then_inc(scaled, 1)
                dve.wait_ge(scaled, k + 1)
                c0 = first_mod * KD + k
                dve.tensor_scalar(tmp[:, k % 4, :], tmp[:, k % 4, :], m["mod"][:, c0:c0 + 1], None,
                                  ALU.add).then_inc(shifted, 1)

        @blk.gpsimd
        def _(pool):
            for k in range(KD):
                pool.wait_ge(hi_ready, k + 1)
                pool.tensor_tensor(m["h_lo"][:, k, :], tmp[:, k % 4, :], m["h_hi"][:, k, :].bitcast(F32),
                                   ALU.subtract).then_inc(lo_ready, 1)


def stage_rwkv(nc, mem, m, d):
    NU, PU = 8, 6
    NL = len(LEVELS)
    names = ("low_scaled", "low_shifted", "low_ready", "up_loaded", "up_done", "gates_read",
             "scaled", "shifted", "kk_raw", "kk_sq", "ss_sum", "ss_max", "norm", "norm_inv", "kk",
             "scan", "scan_x", "e_in", "e_ex", "e_inv", "kfac", "k2", "rk", "rk_sum", "bonus", "b", "rt", "at",
             "kbd", "bbd", "abd", "vbd", "tr_done", "tr_read", "prod_done", "ab", "ak", "rb", "rk_t",
             "amat", "x1", "x0", "xt0", "xt1", "tp", "t", "xp", "x", "xt", "wp", "w", "up", "u", "sd", "sp", "s",
             "yp", "y", "mean", "dev", "dev_sq", "var", "gstd", "grstd", "yn", "ya", "yb", "pair_done", "zeroed",
             "dc")
    with nc.cleanup_on_exit(), ExitStack() as ctx:
        s = {n: nc.alloc_semaphore("rw_" + n) for n in names}
        s.update(ring_sems(nc, ctx, "rw"))
        z = m["z"]
        r, k, v, sw, L, a, kk, t1 = (z[:, 8 + n, :] for n in range(8))
        lat3, at = mem.put("rw_lat", [P, 3, T], F32, mem.work)
        lat = [lat3[:, n, :] for n in range(3)] + [z[:, NPAIR - 2, :]]
        low = z[:, NPAIR - 1, :].rearrange("p (a n) -> p a n", a=4)
        t2, at = mem.put("rw_t2", [P, T], F32, at)
        ARs, at = mem.put("rw_AR", [P, 2, NCH * 2, CH], F32, at)
        Abds, at = mem.put("rw_Abd", [P, 2, NCH, P], F32, at)
        gs, at = mem.put("rw_g", [P, 2, T], F32, at)
        bonus, at = mem.put("rw_bonus", [P, 2, T], F32, at)
        dCs, at = mem.put("rw_dC", [P, 2, NCH], F32, at)
        Kbd, at = mem.put("rw_Kbd", [P, NCH, P], F32, at)
        Bbd, at = mem.put("rw_Bbd", [P, NCH, P], F32, at)
        Vbd, at = mem.put("rw_Vbd", [P, NCH, P], F32, at)
        XT, at = mem.put("rw_XT", [P, NCH, P], F32, at)
        Kt, at = mem.put("rw_Kt", [P, NCH, P], F32, at)
        Bt, at = mem.put("rw_Bt", [P, NCH, P], F32, at)
        Vt, at = mem.put("rw_Vt", [P, NCH, P], F32, at)
        AbT, at = mem.put("rw_AbT", [P, NCH, P], F32, at)
        AkT, at = mem.put("rw_AkT", [P, NCH, P], F32, at)
        RbT, at = mem.put("rw_RbT", [P, NCH, CH], F32, at)
        RkT, at = mem.put("rw_RkT", [P, NCH, CH], F32, at)
        S, at = mem.put("rw_S", [P, 2, P], F32, at)
        Sd, at = mem.put("rw_Sd", [P, P], F32, at)
        W, at = mem.put("rw_W", [P, P], F32, at)
        U, at = mem.put("rw_U", [P, P], F32, at)
        X, TT = Kbd, Vbd
        bank = m["bank"]
        prj = bank[0:3]
        chain, ybank = bank[3], bank[7]
        wcol, ucol, scol = (chain[:, n * P:(n + 1) * P] for n in range(3))
        HALF = (slice(0, CH), slice(CH, P))
        SHARE = [2] * 10 + [1] * 22 + [0] * 2 + [3] * 2
        assert sum(SHARE) == 8 * PU
        blk = ctx.enter_context(nc.Block())

        def chunks(ap):
            return ap.rearrange("p (c t) -> p c t", t=CH)

        def four(b):
            return b[:].rearrange("p (c t) -> p c t", t=P)

        def AR(q):
            return ARs[:, q, :, :].rearrange("p (c x) t -> p c x t", x=2)

        def in_turn(eng, pair):
            with eng.Fori(0, NPAIR // 2 - 1) as i:
                for q in range(2):
                    pair(i * 2 + q, q, True, True)
            pair(NPAIR - 2, 0, True, False)
            pair(NPAIR - 1, 1, False, False)

        @blk.sync
        def _(sp):
            def load_pair(p):
                for j in range(PU):
                    load_unit(sp, m, s, p * PU + (NU + j), j % 2, p * (PU // 2) + (NU // 2 + j // 2),
                              row(d["w_in"], p * PU + (NU + j)), UNIT)

            def load_low(p):
                sp.wait_ge(s["up_done"], p + 1)
                sp.dma_start(low, row(d["low"], p).rearrange("p (a n) -> p a n", a=4)).then_inc(s["up_loaded"], 16)

            for u in range(NU):
                load_unit(sp, m, s, u, u % 2, u // 2, d["w_in"][u], UNIT)
            load_low(0)
            load_pair(0)
            load_pair(1)

            def pair(p, q, ahead, ahead2):
                if ahead:
                    load_low(p + 1)
                if ahead2:
                    load_pair(p + 2)

            in_turn(sp, pair)

        @blk.gpsimd
        def _(pool):
            pool.sem_inc(s["lo_ready"], 2)
            for tile in (Abds, Kbd, Bbd, Vbd, AbT, AkT):
                pool.memset(tile[:], 0.0).then_inc(s["zeroed"], 1)
            for u in range(NU + 2 * PU):
                remainder_unit(pool, m, s, u, u % 2, UNIT)
            with pool.Fori(2, NPAIR) as p:
                for j in range(PU):
                    remainder_unit(pool, m, s, p * PU + (NU + j), j % 2, UNIT)

        @blk.scalar
        def _(act):
            def round_pair(p, j):
                round_unit(act, m, s, p * PU + (NU + j), j % 2, p * (PU // 2) + (NU // 2 + j // 2), UNIT)

            def unshifted(p):
                for n, dst in enumerate((r, k, v)):
                    tile_done(act, s, p * PU + (NU + 2 * n + 1))
                    act.activation(dst, prj[n][:], ACT.Identity,
                                   scale=m["omm"][:, bass.ds(p + 8 * n, 1)]).then_inc(s["scaled"], 1)

            def prepare(p, q, part):
                if part == 0:
                    act.wait_ge(s["up_done"], p + 2)
                    act.activation(sw, bank[4][:], ACT.Sigmoid, bias=vec(m, "w0", p)).then_inc(s["gates_read"], 1)
                    act.activation(a, bank[5][:], ACT.Sigmoid, bias=vec(m, "a0", p)).then_inc(s["gates_read"], 1)
                    act.activation(gs[:, q, :], bank[6][:], ACT.Copy).then_inc(s["gates_read"], 1)
                if part == 1:
                    act.wait_ge(s["kk_raw"], p + 1)
                    act.activation(t2[:], kk, ACT.Square).then_inc(s["kk_sq"], 1)
                if part == 2:
                    act.wait_ge(s["scan_x"], p + 1)
                    act.activation(sw, L, ACT.Exp, scale=-DECAY_C).then_inc(s["e_in"], 1)
                    act.activation(t1, t1, ACT.Exp, scale=-DECAY_C).then_inc(s["e_ex"], 1)
                if part == 3:
                    act.wait_ge(s["e_in"], p + 1)
                    act.activation(L, L, ACT.Exp, scale=DECAY_C).then_inc(s["e_inv"], 1)
                    act.activation(dCs[:, q, :], chunks(sw)[:, :, CH - 1], ACT.Copy).then_inc(s["dc"], 1)
                    act.wait_ge(s["ss_max"], p + 1)
                    act.activation(t2[:], t2[:], ACT.Sqrt).then_inc(s["norm"], 1)
                if part == 5:
                    act.wait_ge(s["shifted"], p * 3 + 3)
                    for h in HALF:
                        act.activation(Vbd[h, :, h], chunks(v)[h], ACT.Copy).then_inc(s["vbd"], 1)
                if part == 7:
                    act.wait_ge(s["at"], p + 1)
                    for h in HALF:
                        act.activation(Abds[h, q, :, h], AR(q)[h, :, 0, :], ACT.Copy).then_inc(s["abd"], 1)

            for u in range(NU):
                round_unit(act, m, s, u, u % 2, u // 2, UNIT)
                if u % 2 == 1:
                    t = u // 2
                    tile_done(act, s, u)
                    act.activation(lat[t], bank[t][:], ACT.Identity,
                                   scale=m["omm"][:, 24 + t:25 + t]).then_inc(s["low_scaled"], 1)
            for j in range(2):
                round_pair(0, j)
            for t, f in enumerate((ACT.Sigmoid, ACT.Sigmoid, ACT.Tanh)):
                act.wait_ge(s["low_shifted"], t + 1)
                act.activation(lat[t], lat[t], f).then_inc(s["low_ready"], 1)
            act.wait_ge(s["zeroed"], 6)
            for j in range(2, PU):
                round_pair(0, j)
            unshifted(0)
            for part in range(8):
                if part < PU:
                    round_pair(1, part)
                prepare(0, 0, part)

            def pair(p, q, ahead, ahead2):
                for n, dst in enumerate((Kt, Bt, Vt)):
                    for o in range(2):
                        act.wait_ge(s["tr_done"], p * 6 + (2 * n + o + 1))
                        act.activation(dst[:, 4 * o:4 * o + 4, :], four(bank[3 + (2 * n + o) % 4]),
                                       ACT.Copy).then_inc(s["tr_read"], 1)
                if ahead2:
                    round_pair(p + 2, 0)
                if ahead:
                    unshifted(p + 1)
                if ahead2:
                    for j in (1, 2, 3):
                        round_pair(p + 2, j)
                for c in range(NCH):
                    act.wait_ge(s["wp"], p * NCH + (c + 1))
                    act.activation(W[:], wcol, ACT.Copy).then_inc(s["w"], 1)
                    if c:
                        act.wait_ge(s["s"], p * NCH + c)
                        act.activation(Sd[:], S[:, c % 2, :], ACT.Copy, scale=dCs[:, q, c:c + 1]).then_inc(s["sd"], 1)
                    act.wait_ge(s["up"], p * NCH + (c + 1))
                    act.activation(U[:], ucol, ACT.Copy).then_inc(s["u"], 1)
                    if ahead2 and c in (1, 3):
                        round_pair(p + 2, {1: 4, 3: 5}[c])
                    if ahead:
                        prepare(p + 1, 1 - q, c)
                act.wait_ge(s["yp"], p * NCH + NCH)
                act.activation(row(z, p, 1), ybank[:], ACT.Copy).then_inc(s["y"], 1)
                act.wait_ge(s["dev"], p + 1)
                act.activation(t1, t2[:], ACT.Square).then_inc(s["dev_sq"], 1)
                act.wait_ge(s["var"], p + 1)
                act.activation(t1, ybank[:], ACT.Sqrt, bias=m["eps"][:, 1:2], scale=1.0 / CH).then_inc(s["gstd"], 1)

            in_turn(act, pair)

        @blk.vector
        def _(dve):
            def shift(p):
                for n, dst in enumerate((r, k, v)):
                    dve.wait_ge(s["scaled"], p * 3 + (n + 1))
                    dve.scalar_tensor_tensor(out=dst[:, 1:T], in0=prj[n][:, 0:T - 1], scalar=vec(m, "mu", p + 8 * n),
                                             in1=dst[:, 1:T], op0=ALU.mult, op1=ALU.add).then_inc(s["shifted"], 1)

            def prepare(p, q, part):
                def after(name, i=0, n=1):
                    dve.wait_ge(s[name], p * n + (i + 1))

                if part == 0:
                    after("shifted", 1, 3)
                    dve.tensor_scalar(kk, k, vec(m, "k_k", p), None, ALU.mult).then_inc(s["kk_raw"], 1)
                if part == 1:
                    after("gates_read", 2, 3)
                    dve.tensor_tensor_scan(L, con(m, "reset", T), sw, 0.0, ALU.mult, ALU.add).then_inc(s["scan"], 1)
                    after("scan")
                    dve.tensor_tensor(t1, L, sw, ALU.subtract).then_inc(s["scan_x"], 1)
                if part == 2:
                    after("ss_sum")
                    dve.tensor_scalar(t2[:], bank[4][:], 1e-24, None, ALU.max).then_inc(s["ss_max"], 1)
                if part == 3:
                    after("norm")
                    dve.reciprocal(t2[:], t2[:]).then_inc(s["norm_inv"], 1)
                if part == 4:
                    after("norm_inv")
                    dve.tensor_tensor(kk, kk, t2[:], ALU.mult).then_inc(s["kk"], 1)
                    after("kk")
                    dve.tensor_scalar(t2[:], a, -1.0, vec(m, "k_a", p), ALU.add, ALU.mult).then_inc(s["kfac"], 1)
                    after("kfac")
                    dve.scalar_tensor_tensor(out=k, in0=t2[:], scalar=1.0, in1=k, op0=ALU.add,
                                             op1=ALU.mult).then_inc(s["k2"], 1)
                if part == 5:
                    after("k2")
                    dve.scalar_tensor_tensor(out=t2[:], in0=r, scalar=vec(m, "r_k", p), in1=k,
                                             op0=ALU.mult, op1=ALU.mult).then_inc(s["rk"], 1)
                    dve.tensor_tensor(a, kk, a, ALU.mult).then_inc(s["b"], 1)
                    after("e_in")
                    dve.tensor_tensor(AR(q)[:, :, 1, :], chunks(r), chunks(sw), ALU.mult).then_inc(s["rt"], 1)
                if part == 6:
                    after("e_ex")
                    dve.scalar_tensor_tensor(out=AR(q)[:, :, 0, :], in0=chunks(kk), scalar=-1.0, in1=chunks(t1),
                                             op0=ALU.mult, op1=ALU.mult).then_inc(s["at"], 1)
                    after("e_inv")
                    after("b")
                    for h in HALF:
                        dve.tensor_tensor(Kbd[h, :, h], chunks(k)[h], chunks(L)[h], ALU.mult).then_inc(s["kbd"], 1)
                if part == 7:
                    after("rk_sum")
                    dve.tensor_tensor(bonus[:, q, :], bank[5][:], v, ALU.mult).then_inc(s["bonus"], 1)
                    for h in HALF:
                        dve.tensor_tensor(Bbd[h, :, h], chunks(a)[h], chunks(L)[h], ALU.mult).then_inc(s["bbd"], 1)

            for t in range(4):
                dve.wait_ge(s["low_scaled"], t + 1)
                dve.scalar_tensor_tensor(out=lat[t][:, 1:T], in0=bank[t][:, 0:T - 1], scalar=vec(m, "mu", 24 + t),
                                         in1=lat[t][:, 1:T], op0=ALU.mult, op1=ALU.add).then_inc(s["low_shifted"], 1)
            dve.wait_ge(s["zeroed"], 6)
            shift(0)
            for part in range(8):
                prepare(0, 0, part)

            def pair(p, q, ahead, ahead2):
                def after(name, i=0, n=1):
                    dve.wait_ge(s[name], p * n + (i + 1))

                for o in range(4):
                    after("prod_done", o, 4)
                    pr = bank[3 + o][:].rearrange("p (c x t) -> p c x t", c=2, x=4)
                    cc = slice(2 * o, 2 * o + 2)
                    for h in HALF:
                        dve.tensor_tensor(AbT[h, cc, h], pr[h, :, 0, :], over(con(m, "below", CH)[h], 2),
                                          ALU.mult).then_inc(s["ab"], 1)
                    for h in HALF:
                        dve.tensor_tensor(AkT[h, cc, h], pr[h, :, 2, :], over(con(m, "below", CH)[h], 2),
                                          ALU.mult).then_inc(s["ak"], 1)
                    dve.tensor_tensor(RbT[:, cc, :], pr[:, :, 1, :], over(con(m, "upto", CH), 2),
                                      ALU.mult).then_inc(s["rb"], 1)
                    dve.tensor_tensor(RkT[:, cc, :], pr[:, :, 3, :], over(con(m, "upto", CH), 2),
                                      ALU.mult).then_inc(s["rk_t"], 1)
                after("ab", 7, 8)
                dve.tensor_tensor(XT[:], AbT[:], over(con(m, "m1t"), NCH), ALU.mult).then_inc(s["xt0"], 1)
                for o in range(2):
                    cc = slice(4 * o, 4 * o + 4)
                    after("amat", o, 2)
                    dve.tensor_tensor(X[:, cc, :], four(bank[3 + 2 * o]), over(con(m, "m1"), 4),
                                      ALU.mult).then_inc(s["x0"], 1)
                    after("x0", o, 2)
                    dve.tensor_tensor(X[:, cc, :], X[:, cc, :], over(con(m, "ident"), 4),
                                      ALU.add).then_inc(s["x1"], 1)
                after("xt0")
                dve.tensor_tensor(XT[:], XT[:], over(con(m, "ident"), NCH), ALU.add).then_inc(s["xt1"], 1)
                if ahead:
                    shift(p + 1)
                for l, b in enumerate(LEVELS):
                    for o in range(2):
                        after("tp", 2 * l + o, 2 * NL)
                        dve.tensor_tensor(TT[:, 4 * o:4 * o + 4, :], four(bank[3 + 2 * o]), over(con(m, f"m{b}"), 4),
                                          ALU.mult).then_inc(s["t"], 1)
                    for o in range(2):
                        cc = slice(4 * o, 4 * o + 4)
                        after("xp", 2 * l + o, 2 * NL)
                        if l:
                            after("xt", 2 * (l - 1) + o, 2 * NL)
                        if l < NL - 1:
                            dve.tensor_tensor(X[:, cc, :], four(bank[3 + 2 * o]), X[:, cc, :],
                                              ALU.add).then_inc(s["x"], 1)
                        dve.tensor_tensor(XT[:, cc, :], four(bank[4 + 2 * o]), XT[:, cc, :],
                                          ALU.add).then_inc(s["xt"], 1)
                for c in range(NCH):
                    after("sp", c, NCH)
                    if c:
                        after("yp", c - 1, NCH)
                        after("sd", c - 1, NCH - 1)
                        dve.scalar_tensor_tensor(out=S[:, (c + 1) % 2, :], in0=scol, scalar=dCs[:, q, c:c + 1],
                                                 in1=Sd[:], op0=ALU.mult, op1=ALU.add).then_inc(s["s"], 1)
                    else:
                        after("dc")
                        dve.tensor_scalar(S[:, 1, :], scol, dCs[:, q, 0:1], None, ALU.mult).then_inc(s["s"], 1)
                    if ahead:
                        prepare(p + 1, 1 - q, c)
                zp = row(z, p, 1)
                after("mean")
                dve.scalar_tensor_tensor(out=t2[:], in0=ybank[:], scalar=-1.0 / CH, in1=zp, op0=ALU.mult,
                                         op1=ALU.add).then_inc(s["dev"], 1)
                after("gstd")
                dve.reciprocal(t1, t1).then_inc(s["grstd"], 1)
                after("grstd")
                dve.tensor_tensor(t2[:], t2[:], t1, ALU.mult).then_inc(s["yn"], 1)
                after("yn")
                dve.tensor_scalar(t2[:], t2[:], vec(m, "ln_g", p), vec(m, "ln_b", p), ALU.mult,
                                  ALU.add).then_inc(s["ya"], 1)
                after("ya")
                dve.tensor_tensor(t2[:], t2[:], bonus[:, q, :], ALU.add).then_inc(s["yb"], 1)
                after("yb")
                dve.tensor_tensor(zp, t2[:], gs[:, q, :], ALU.mult).then_inc(s["pair_done"], 1)

            in_turn(dve, pair)

        @blk.tensor
        def _(pe):
            def project(p, j):
                multiply_unit(pe, m, s, p * PU + (NU + j), j % 2, prj[j // 2][:], m["h_hi"], m["h_lo"], 8 * (j % 2), 8,
                              j % 2 == 0, j % 2 == 1)

            def fill(p, gap):
                for kt in range(sum(SHARE[:gap]), sum(SHARE[:gap + 1])):
                    j = kt // 8
                    if kt % 16 == 0:
                        pe.wait_ge(s["shifted"], p * 3 + (j // 2 - 2))
                    multiply_part(pe, m, s, p * PU + (NU + j), j % 2, prj[j // 2][:], m["h_hi"], m["h_lo"],
                                  8 * (j % 2), kt % 8, 1, 8, j % 2 == 0, j % 2 == 1)

            def prepare(p, part):
                if part == 0:
                    pe.wait_ge(s["up_loaded"], p * 16 + 16)
                    pe.matmul(bank[4][:], low[:, 2, :], lat[2], start=True, stop=True)
                    pe.matmul(bank[5][:], low[:, 3, :], lat[3], start=True, stop=True)
                    pe.matmul(bank[6][:], low[:, 0, :], lat[0], start=True, stop=False)
                    pe.matmul(bank[6][:], low[:, 1, :], lat[1], start=False, stop=True).then_inc(s["up_done"], 1)
                if part == 2:
                    pe.wait_ge(s["kk_sq"], p + 1)
                    pe.matmul(bank[4][:], con(m, "heads"), t2[:], start=True, stop=True).then_inc(s["ss_sum"], 1)
                if part == 6:
                    pe.wait_ge(s["rk"], p + 1)
                    pe.matmul(bank[5][:], con(m, "heads"), t2[:], start=True, stop=True).then_inc(s["rk_sum"], 1)

            pe.sem_inc(s["unit_used"], 2)
            pe.sem_inc(s["up_done"], 1)
            for u in range(NU):
                multiply_unit(pe, m, s, u, u % 2, bank[u // 2][:], m["h_hi"], m["h_lo"], 8 * (u % 2), 8,
                              u % 2 == 0, u % 2 == 1)
            pe.wait_ge(s["low_shifted"], 4)
            for j in range(PU):
                project(0, j)
            pe.wait_ge(s["low_ready"], 3)
            for part in range(8):
                prepare(0, part)
                if part < PU:
                    if part % 2 == 0:
                        pe.wait_ge(s["shifted"], part // 2 + 1)
                    project(1, part)

            def pair(p, q, ahead, ahead2):
                def after(name, i=0, n=1):
                    pe.wait_ge(s[name], p * n + (i + 1))

                def each(lhsT, rhs, b, o):
                    for n in range(4):
                        mm = pe.matmul(bank[b][:, n * P:(n + 1) * P], lhsT[:, 4 * o + n, :], rhs(4 * o + n),
                                       start=True, stop=True)
                    return mm

                for n, (tile, name) in enumerate(((Kbd, "kbd"), (Bbd, "bbd"), (Vbd, "vbd"))):
                    after(name, 1, 2)
                    for o in range(2):
                        if 2 * n + o == 2:
                            after("bonus")
                        if 2 * n + o >= 4:
                            after("tr_read", 2 * n + o - 4, 6)
                        for i in range(4):
                            mm = pe.transpose(bank[3 + (2 * n + o) % 4][:, i * P:(i + 1) * P], tile[:, 4 * o + i, :],
                                              con(m, "ident"))
                        mm.then_inc(s["tr_done"], 1)
                after("rt")
                after("at")
                for o in range(4):
                    after("tr_read", o + 2 if o > 1 else o + 4, 6)
                    for c in (2 * o, 2 * o + 1):
                        w = (c % 2) * 2 * P
                        ar = AR(q)[:, c, :, :].rearrange("p x t -> p (x t)")
                        pe.matmul(bank[3 + o][:, w:w + P], Bbd[:, c, :], ar, start=True, stop=True)
                        mm = pe.matmul(bank[3 + o][:, w + P:w + 2 * P], Kbd[:, c, :], ar, start=True, stop=True)
                    mm.then_inc(s["prod_done"], 1)
                for o in range(2):
                    after("rk_t", 2 * o + 1, 4)
                    each(AbT, lambda c: con(m, "ident"), 3 + 2 * o, o).then_inc(s["amat"], 1)
                for l in range(NL):
                    for o in range(2):
                        if l:
                            after("x", 2 * (l - 1) + o, 2 * (NL - 1))
                        else:
                            after("x1", o, 2)
                        each(AbT, lambda c: X[:, c, :], 3 + 2 * o, o).then_inc(s["tp"], 1)
                    if ahead2:
                        fill(p + 2, 2 * l)
                    if l == 0:
                        after("xt1")
                    else:
                        after("xt", 2 * l - 1, 2 * NL)
                    for o in range(2):
                        after("t", 2 * l + o, 2 * NL)
                        if l < NL - 1:
                            each(XT, lambda c: TT[:, c, :], 3 + 2 * o, o)
                        each(TT, lambda c: XT[:, c, :], 4 + 2 * o, o).then_inc(s["xp"], 1)
                    if ahead2:
                        fill(p + 2, 2 * l + 1)
                after("xt", 2 * NL - 1, 2 * NL)
                after("abd", 1, 2)
                for c in range(NCH):
                    if ahead:
                        prepare(p + 1, c)
                    if c:
                        after("s", c - 1, NCH)
                    w = pe.matmul(wcol, AkT[:, c, :], Vt[:, c, :], start=True, stop=c == 0)
                    if c:
                        w = pe.matmul(wcol, Abds[:, q, c, :], S[:, c % 2, :], start=False, stop=True)
                    w.then_inc(s["wp"], 1)
                    if ahead2:
                        fill(p + 2, 10 + 3 * c)
                    after("w", c, NCH)
                    pe.matmul(ucol, XT[:, c, :], W[:], start=True, stop=True).then_inc(s["up"], 1)
                    if ahead2:
                        fill(p + 2, 10 + 3 * c + 1)
                    after("u", c, NCH)
                    pe.matmul(scol, Kt[:, c, :], Vt[:, c, :], start=True, stop=False)
                    pe.matmul(scol, Bt[:, c, :], U[:], start=False, stop=True).then_inc(s["sp"], 1)
                    y = ybank[:, c * CH:(c + 1) * CH]
                    if c:
                        pe.matmul(y, S[:, c % 2, :], AR(q)[:, c, 1, :], start=True, stop=False)
                    pe.matmul(y, Vt[:, c, :], RkT[:, c, :], start=c == 0, stop=False)
                    pe.matmul(y, U[:], RbT[:, c, :], start=False, stop=True).then_inc(s["yp"], 1)
                    if ahead2:
                        fill(p + 2, 10 + 3 * c + 2)
                after("y")
                pe.matmul(ybank[:], con(m, "heads"), row(z, p, 1), start=True, stop=True).then_inc(s["mean"], 1)
                if ahead2:
                    fill(p + 2, 34)
                after("dev_sq")
                pe.matmul(ybank[:], con(m, "heads"), t1, start=True, stop=True).then_inc(s["var"], 1)
                if ahead2:
                    fill(p + 2, 35)

            in_turn(pe, pair)


def stage_latents(nc, mem, m, d):
    NT = LATQ + LATKV + 1
    NU = 2 * NT
    NB, MOD0 = 4, 4
    names = ("copied", "ang", "sq", "sum", "root", "rstd", "scaled", "sin_in", "sin_out",
             "pos", "swapped", "rot", "loads")
    with nc.cleanup_on_exit(), ExitStack() as ctx:
        s = {n: nc.alloc_semaphore("lt_" + n) for n in names}
        s.update(ring_sems(nc, ctx, "lt"))
        s.update(mod_sems(nc, "lt", NB))
        lat, at = mem.put("mla_lat", [P, NT, T], F32, mem.work)
        cos, at = mem.put("mla_cos", [P, T], F32, at)
        sin, at = mem.put("mla_sin", [P, T], F32, at)
        m["lat"], m["cos"], m["sin"] = lat, cos, sin
        m["attention_work"] = at
        pos, at = mem.put("lt_pos", [P, T], I32, at)
        ang, at = mem.put("lt_ang", [P, T], F32, at)
        turns, at = mem.put("lt_turns", [P, T], F32, at)
        sq, at = mem.put("lt_sq", [P, LATQ + LATKV, T], F32, at)
        rstd, at = mem.put("lt_rstd", [P, 2, T], F32, at)
        rot, at = mem.put("lt_rot", [P, 2, T], F32, at)
        mbuf, at = mem.put("lt_mod_buf", [P, NB, GRP], F32, at)
        macc, at = mem.put("lt_mod_acc", [P, 2, GRP], F32, at)
        rest = rot[:, 0, :]
        bank = m["bank"]
        base = 56
        groups = ((0, LATQ, "q_g"), (LATQ, LATKV, "kv_g"))
        blk = ctx.enter_context(nc.Block())

        @blk.sync
        def _(sp):
            sp.dma_start(pos[:], d["pos"]).then_inc(s["loads"], 16)
            for u in range(2 * KD):
                if u < NU:
                    load_unit(sp, m, s, u, u % 2, u // 2, d["w_in"][base + u], UNIT)
                load_mod(sp, s, mbuf, u, u % NB, mod_unit(d, MOD0 * KD + u))

        @blk.gpsimd
        def _(pool):
            pool.sem_inc(s["lo_ready"], 2)
            for u in range(NU):
                remainder_unit(pool, m, s, u, u % 2, UNIT)

        @blk.tensor
        def _(pe):
            pe.sem_inc(s["unit_used"], 2)
            for u in range(NU):
                multiply_unit(pe, m, s, u, u % 2, bank[u // 2][:], m["h_hi"], m["h_lo"], 8 * (u % 2), 8,
                              u % 2 == 0, u % 2 == 1)
            for n, (t0, nt, _) in enumerate(groups):
                for t in range(t0, t0 + nt):
                    pe.wait_ge(s["sq"], t + 1)
                    mm = pe.matmul(bank[n][:], con(m, "ones"), sq[:, t, :], start=t == t0, stop=t == t0 + nt - 1)
                mm.then_inc(s["sum"], 1)
            for g in range(2):
                mod_columns(pe, m, s, bank[7], macc[:, g, :], (MOD0 + g) * (GRP // P), KD * (g + 1) + NB)
            pe.wait_ge(s["copied"], NT)
            pe.matmul(bank[2][:], con(m, "swap"), lat[:, NT - 1, :], start=True, stop=True).then_inc(s["swapped"], 1)

        def copy_tile(act, t):
            tile_done(act, s, 2 * t + 1)
            act.activation(lat[:, t, :], bank[t][:], ACT.Copy).then_inc(s["copied"], 1)

        @blk.scalar
        def _(act):
            for u in range(NU):
                round_unit(act, m, s, u, u % 2, u // 2, UNIT)
                if u % 2 and u // 2:
                    copy_tile(act, u // 2 - 1)
            copy_tile(act, NT - 1)
            for t in range(LATQ + LATKV):
                act.wait_ge(s["copied"], t + 1)
                act.activation(sq[:, t, :], lat[:, t, :], ACT.Square).then_inc(s["sq"], 1)
            for n, (t0, nt, _) in enumerate(groups):
                act.wait_ge(s["sum"], n + 1)
                act.activation(rstd[:, n, :], bank[n][:], ACT.Sqrt, bias=m["eps"][:, 0:1],
                               scale=1.0 / (nt * P)).then_inc(s["root"], 1)
            act.wait_ge(s["sin_in"], 2)
            act.activation(sin[:], ang[:], ACT.Sin).then_inc(s["sin_out"], 1)
            act.activation(cos[:], turns[:], ACT.Sin, bias=m["eps"][:, 2:3], scale=-1.0).then_inc(s["sin_out"], 1)

        @blk.vector
        def _(dve):
            dve.sem_inc(s["mod_summed"], NB)
            dve.sem_inc(s["mod_cols"], 2)
            dve.wait_ge(s["loads"], 16)
            dve.tensor_copy(ang[:], pos[:]).then_inc(s["pos"], 1)
            dve.wait_ge(s["pos"], 1)
            dve.tensor_scalar(ang[:], ang[:], con(m, "freq", 1), None, ALU.mult).then_inc(s["ang"], 1)
            steps = [1]

            def step(op):
                steps[0] += 1
                op.then_inc(s["ang"], 1)
                dve.wait_ge(s["ang"], steps[0])

            def less(acc, part, e):
                step(dve.scalar_tensor_tensor(out=acc, in0=turns[:], scalar=-part * 2.0 ** e, in1=acc,
                                              op0=ALU.mult, op1=ALU.add))

            big = 1.5 * 2.0 ** 23
            parts = two_pi_parts()
            dve.wait_ge(s["ang"], 1)
            step(dve.memset(rest, 0.0))
            for e in (22, 11):
                step(dve.tensor_scalar(turns[:], ang[:], 1.0 / (2 * math.pi * 2 ** e), -0.5, ALU.mult, ALU.add))
                step(dve.tensor_scalar(turns[:], turns[:], big, None, ALU.add))
                step(dve.tensor_scalar(turns[:], turns[:], -big, None, ALU.add))
                for n, part in enumerate(parts):
                    less(ang[:] if n < 2 else rest, part, e)
            step(dve.tensor_tensor(turns[:], ang[:], rest, ALU.add))
            step(dve.tensor_scalar(turns[:], turns[:], 1.0 / (2 * math.pi), big, ALU.mult, ALU.add))
            step(dve.tensor_scalar(turns[:], turns[:], -big, None, ALU.add))
            less(ang[:], parts[0], 0)
            less(ang[:], parts[1], 0)
            step(dve.tensor_tensor(ang[:], ang[:], rest, ALU.add))
            less(ang[:], parts[2], 0)
            less(ang[:], parts[3], 0)
            dve.tensor_scalar(ang[:], ang[:], float(np.float32(3.1415925)), -float(np.float32(3.1415925)),
                              ALU.min, ALU.max).then_inc(s["sin_in"], 1)
            dve.wait_ge(s["sin_in"], 1)
            dve.scalar_tensor_tensor(out=turns[:], in0=ang[:], scalar=-1.0, in1=ang[:], op0=ALU.mult,
                                     op1=ALU.max).then_inc(s["sin_in"], 1)
            for u in range(2 * KD):
                add_mod(dve, m, s, mbuf, macc[:, u // KD, :], u, u % NB, u // NB, NB, u % KD, u % KD == 0)
            finish_mod(dve, m, s, bank[7], 2 * KD, KD, 2, (2, "g_post_mix", 2 * KD))
            for n, (t0, nt, g) in enumerate(groups):
                dve.wait_ge(s["root"], n + 1)
                dve.reciprocal(rstd[:, n, :], rstd[:, n, :]).then_inc(s["rstd"], 1)
                dve.wait_ge(s["rstd"], n + 1)
                for t in range(t0, t0 + nt):
                    dve.scalar_tensor_tensor(out=lat[:, t, :], in0=lat[:, t, :], scalar=vec(m, g, t - t0),
                                             in1=rstd[:, n, :], op0=ALU.mult, op1=ALU.mult)
            dve.wait_ge(s["sin_out"], 2)
            dve.wait_ge(s["swapped"], 1)
            dve.tensor_tensor(rot[:, 0, :], lat[:, NT - 1, :], cos[:], ALU.mult).then_inc(s["rot"], 1)
            dve.tensor_tensor(rot[:, 1, :], bank[2][:], sin[:], ALU.mult).then_inc(s["rot"], 1)
            dve.wait_ge(s["rot"], 2)
            dve.tensor_tensor(lat[:, NT - 1, :], rot[:, 0, :], rot[:, 1, :], ALU.add).then_inc(s["rot"], 1)


def two_pi_parts():
    left, parts = 2 * math.pi, []
    for _ in range(4):
        e = math.floor(math.log2(abs(left))) - 10
        part = math.floor(left / 2.0 ** e) * 2.0 ** e
        parts.append(part)
        left -= part
    parts[-1] += left
    return parts


def stage_attention(nc, mem, m, d):
    NH2 = 4
    QW, KW = LATQ * 3 * P, LATKV * 2 * P
    names = ("w_loaded", "proj", "q_copied", "swapped", "rot", "v_copied", "zeroed", "score", "max", "neg", "exp",
             "inv", "prob", "turned", "pt", "out", "y", "w_used")
    with nc.cleanup_on_exit(), ExitStack() as ctx:
        s = {n: nc.alloc_semaphore("at_" + n) for n in names}
        wq, at = mem.put("at_wq", [P, LATQ, 3 * P], F32, mem.h)
        wk, at = mem.put("at_wk", [P, LATKV, 2 * P], F32, at)
        wv, at = mem.put("at_wv", [P, LATKV, 2 * P], F32, at)
        q, at = mem.put("at_q", [P, 2, T], F32, at)
        qr, at = mem.put("at_qr", [P, T], F32, at)
        rot, at = mem.put("at_rot", [P, 2, T], F32, at)
        qh, at = mem.put("at_qh", [P, 2, T], F32, at)
        k, at = mem.put("at_k", [P, 2, T], F32, at)
        v, at = mem.put("at_v", [P, 4, 2 * P], F32, at)
        pr, at = mem.put("at_p", [P, 4, T], F32, at)
        pt, at = mem.put("at_pt", [P, 4, T], F32, at)
        nmax, at = mem.put("at_nmax", [P, 4], F32, at)
        den, at = mem.put("at_den", [P, 4], F32, at)
        lat, cos, sin = m["lat"], m["cos"], m["sin"]
        kr = lat[:, LATQ + LATKV, :]
        bank = m["bank"]
        z = m["z"]
        HALF = (slice(0, CH), slice(CH, P))
        blk = ctx.enter_context(nc.Block())

        @blk.sync
        def _(sp):
            with sp.Fori(0, NH2) as i:
                sp.wait_ge(s["w_used"], i + 1)
                for tile, n in ((wq, "w_q"), (wk, "w_k"), (wv, "w_v")):
                    w = tile.shape[2]
                    sp.dma_start(tile[:], row(d[n], i).rearrange("p (a n) -> p a n", n=w)).then_inc(s["w_loaded"], 16)

        @blk.gpsimd
        def _(pool):
            pool.memset(qh[:], 0.0).then_inc(s["zeroed"], 1)

        @blk.tensor
        def _(pe):
            pe.sem_inc(s["w_used"], 1)
            pe.wait_ge(s["zeroed"], 1)
            with pe.Fori(0, NH2) as i:
                pe.wait_ge(s["w_loaded"], i * 48 + 48)
                pe.wait_ge(s["y"], i * 2 + 1)
                for t in range(3):
                    for c in range(LATQ):
                        mm = pe.matmul(bank[4 + t][:], wq[:, c, t * P:(t + 1) * P], lat[:, c, :],
                                       start=c == 0, stop=c == LATQ - 1)
                    mm.then_inc(s["proj"], 1)
                for t in range(2):
                    for c in range(LATKV):
                        mm = pe.matmul(bank[(7 + t) % 8][:], wk[:, c, t * P:(t + 1) * P], lat[:, LATQ + c, :],
                                       start=c == 0, stop=c == LATKV - 1)
                    mm.then_inc(s["proj"], 1)
                for t in range(4):
                    for c in range(LATKV):
                        mm = pe.matmul(bank[1 + t // 2][:, (t % 2) * 2 * P:(t % 2 + 1) * 2 * P],
                                       lat[:, LATQ + c, t * P:(t + 1) * P], wv[:, c, :],
                                       start=c == 0, stop=c == LATKV - 1)
                    if t % 2:
                        mm.then_inc(s["proj"], 1)
                pe.wait_ge(s["q_copied"], i * 5 + 3)
                pe.matmul(bank[3][:], con(m, "swap"), qr[:], start=True, stop=True).then_inc(s["swapped"], 1)
                pe.wait_ge(s["rot"], i * 4 + 4)
                pe.wait_ge(s["q_copied"], i * 5 + 5)
                pe.wait_ge(s["v_copied"], i * 2 + 2)
                for h in range(2):
                    for b in range(4):
                        w = (b + 1) * P
                        qs = slice(b * P, (b + 1) * P)
                        if h:
                            pe.wait_ge(s["exp"], i * 8 + (b + 1))
                        pe.matmul(bank[b][:, 0:w], q[:, h, qs], k[:, h, 0:w], start=True, stop=False)
                        pe.matmul(bank[b][:, 0:w], qh[:, h, qs], kr[:, 0:w], start=False, stop=False)
                        pe.matmul(bank[b][:, b * P:w], con(m, "early"), con(m, "late"), start=False,
                                  stop=True).then_inc(s["score"], 1)
                    for b in range(4):
                        pe.wait_ge(s["prob"], i * 8 + (h * 4 + b + 1))
                    for c in range(4):
                        for b in range(c, 4):
                            mm = pe.transpose(bank[4 + c][:, b * P:(b + 1) * P], pr[:, b, c * P:(c + 1) * P],
                                              con(m, "ident"))
                        mm.then_inc(s["turned"], 1)
                    pe.wait_ge(s["pt"], i * 8 + (h * 4 + 4))
                    for c in range(4):
                        mm = pe.matmul(bank[4][:, c * P:T], v[:, c, h * P:(h + 1) * P], pt[:, c, c * P:T],
                                       start=c == 0, stop=c == 3)
                    mm.then_inc(s["out"], 1)
                    if h == 0:
                        pe.wait_ge(s["y"], i * 2 + 2)
                pe.sem_inc(s["w_used"], 1)

        @blk.scalar
        def _(act):
            act.sem_inc(s["y"], 1)
            with act.Fori(0, NH2) as i:
                for t, dst in enumerate((q[:, 0, :], q[:, 1, :], qr[:], k[:, 0, :], k[:, 1, :])):
                    act.wait_ge(s["proj"], i * 7 + (t + 1))
                    act.activation(dst, bank[(4 + t) % 8][:], ACT.Copy).then_inc(s["q_copied"], 1)
                for t in range(2):
                    act.wait_ge(s["proj"], i * 7 + (6 + t))
                    act.activation(v[:, 2 * t:2 * t + 2, :].rearrange("p a n -> p (a n)"), bank[1 + t][:],
                                   ACT.Copy).then_inc(s["v_copied"], 1)
                for h in range(2):
                    for b in range(4):
                        w = (b + 1) * P
                        n = i * 8 + (h * 4 + b + 1)
                        act.wait_ge(s["neg"], n)
                        act.activation(pr[:, b, 0:w], bank[b][:, 0:w], ACT.Exp, bias=nmax[:, b:b + 1], scale=SCALE,
                                       accum_out=den[:, b:b + 1]).then_inc(s["exp"], 1)
                    for c in range(4):
                        act.wait_ge(s["turned"], i * 8 + (h * 4 + c + 1))
                        act.activation(pt[:, c, c * P:T], bank[4 + c][:, c * P:T], ACT.Copy).then_inc(s["pt"], 1)
                    act.wait_ge(s["out"], i * 2 + (h + 1))
                    act.activation(row(z, i * 2 + (8 + h), 1), bank[4][:], ACT.Copy).then_inc(s["y"], 1)

        @blk.vector
        def _(dve):
            with dve.Fori(0, NH2) as i:
                dve.wait_ge(s["q_copied"], i * 5 + 3)
                dve.tensor_tensor(rot[:, 0, :], qr[:], cos[:], ALU.mult).then_inc(s["rot"], 1)
                dve.wait_ge(s["swapped"], i + 1)
                dve.tensor_tensor(rot[:, 1, :], bank[3][:], sin[:], ALU.mult).then_inc(s["rot"], 1)
                dve.wait_ge(s["rot"], i * 4 + 2)
                for h in range(2):
                    dve.tensor_tensor(qh[HALF[h], h, :], rot[HALF[h], 0, :], rot[HALF[h], 1, :],
                                      ALU.add).then_inc(s["rot"], 1)
                for h in range(2):
                    for b in range(4):
                        w = (b + 1) * P
                        n = i * 8 + (h * 4 + b + 1)
                        dve.wait_ge(s["score"], n)
                        dve.tensor_reduce(nmax[:, b:b + 1], bank[b][:, 0:w], AX_X, ALU.max).then_inc(s["max"], 1)
                        dve.wait_ge(s["max"], n)
                        dve.tensor_scalar(nmax[:, b:b + 1], nmax[:, b:b + 1], -SCALE, None,
                                          ALU.mult).then_inc(s["neg"], 1)
                    for b in range(4):
                        w = (b + 1) * P
                        n = i * 8 + (h * 4 + b + 1)
                        dve.wait_ge(s["exp"], n)
                        dve.reciprocal(den[:, b:b + 1], den[:, b:b + 1]).then_inc(s["inv"], 1)
                        dve.wait_ge(s["inv"], n)
                        dve.tensor_scalar(pr[:, b, 0:w], pr[:, b, 0:w], den[:, b:b + 1], None,
                                          ALU.mult).then_inc(s["prob"], 1)


def stage_mix_out(nc, mem, m, d):
    NB, MOD0, MG = 4, 6, 4
    MU = MG
    names = ("y_hi", "y_lo", "copied", "sq", "summed", "root", "rstd", "normed", "x_loaded", "x1", "kept")
    with nc.cleanup_on_exit(), ExitStack() as ctx:
        s = {n: nc.alloc_semaphore("mo_" + n) for n in names}
        s.update(ring_sems(nc, ctx, "mo"))
        s.update(mod_sems(nc, "mo", NB))
        o, at = mem.put("mo_o", [P, KD, T], F32, mem.work)
        sq, at = mem.put("mo_sq", [P, 2, T], F32, at)
        rstd, at = mem.put("mo_rstd", [P, T], F32, at)
        xin, at = mem.put("mo_x", [P, 4, T], F32, at)
        mbuf, at = mem.put("mo_mod_buf", [P, NB, GRP], F32, at)
        macc, at = mem.put("mo_mod_acc", [P, 2, GRP], F32, at)
        z, bank = m["z"], m["bank"]
        x_sem = [nc.alloc_semaphore(f"mo_xin{j}") for j in range(4)]
        blk = ctx.enter_context(nc.Block())

        @blk.sync
        def _(sp):
            for t in range(2):
                for j in range(2):
                    load_unit(sp, m, s, t * 2 + j, j, t, d["w_out"][t * 2 + j], UNIT)

            def load_mods(t):
                for j in range(MU):
                    load_mod(sp, s, mbuf, t * MU + j, j % NB, mod_unit(d, t * MU + (MOD0 * KD + j)))

            with sp.Fori(2, KD) as t:
                load_mods(t - 2)
                for j in range(2):
                    load_unit(sp, m, s, t * 2 + j, j, t, row(d["w_out"], t * 2 + j), UNIT)
            with sp.Fori(KD - 2, KD) as t:
                load_mods(t)
            for t in range(KD):
                if t >= 4:
                    sp.wait_ge(s["x1"], t - 3)
                sp.dma_start(xin[:, t % 4, :], d["xt"][:, t, :]).then_inc(x_sem[t % 4], 16)
            sp.wait_ge(s["x1"], KD)
            sp.dma_start(d["x1"], z[:]).then_inc(s["kept"], 16)
            sp.wait_ge(s["kept"], 16)

        @blk.gpsimd
        def _(pool):
            pool.sem_inc(s["lo_ready"], 2)
            for u in range(2):
                remainder_unit(pool, m, s, u, u % 2, UNIT)
            for t in range(KD):
                pool.wait_ge(s["y_hi"], t + 1)
                pool.tensor_tensor(m["h_lo"][:, t, :], z[:, t, :], m["h_hi"][:, t, :].bitcast(F32),
                                   ALU.subtract).then_inc(s["y_lo"], 1)
            with pool.Fori(1, KD) as t:
                for j in range(2):
                    remainder_unit(pool, m, s, t * 2 + j, j, UNIT)

        @blk.scalar
        def _(act):
            for u in range(2):
                round_unit(act, m, s, u, u, 0, UNIT)
            for t in range(KD):
                act.activation(m["h_hi"][:, t, :], z[:, t, :], ACT.Copy).then_inc(s["y_hi"], 1)
            for t in range(KD):
                if t < KD - 1:
                    for j in range(2):
                        round_unit(act, m, s, 2 * t + 2 + j, j, t + 1, UNIT)
                tile_done(act, s, 2 * t + 1)
                if t >= 2:
                    act.wait_ge(s["summed"], t - 1)
                act.activation(sq[:, t % 2, :], bank[t % 2][:], ACT.Square).then_inc(s["sq"], 1)
            act.wait_ge(s["summed"], KD)
            act.activation(rstd[:], bank[7][:], ACT.Sqrt, bias=m["eps"][:, 0:1], scale=1.0 / D).then_inc(s["root"], 1)

        @blk.vector
        def _(dve):
            dve.sem_inc(s["mod_summed"], NB)
            dve.sem_inc(s["mod_cols"], 2)
            with dve.Fori(0, 2) as i:
                for t in range(KD // 2):
                    for j in range(MU):
                        g, k = (t * MU + j) // KD, (t * MU + j) % KD
                        if k == 0:
                            dve.wait_ge(s["mod_cols"], i * 2 + (g + 1))
                        add_mod(dve, m, s, mbuf, macc[:, g, :], i * (2 * KD) + (t * MU + j), j, i * (KD // 2) + t,
                                NB, k, k == 0)
                    dve.wait_ge(s["sq"], i * (KD // 2) + (t + 1))
                    dve.tensor_copy(row(o, i * (KD // 2) + t, 1), bank[t % 2][:]).then_inc(s["copied"], 1)
            finish_mod(dve, m, s, bank[6], MOD0 * (GRP // P), 2 * KD, MG, (1, "g_pre_ffn", 4 * KD))
            dve.wait_ge(s["root"], 1)
            dve.reciprocal(rstd[:], rstd[:]).then_inc(s["rstd"], 1)
            dve.wait_ge(s["rstd"], 1)
            for t in range(KD):
                dve.scalar_tensor_tensor(out=o[:, t, :], in0=o[:, t, :], scalar=m["gs"][:, 2 * KD + t:2 * KD + t + 1],
                                         in1=rstd[:], op0=ALU.mult, op1=ALU.mult).then_inc(s["normed"], 1)
                dve.wait_ge(s["normed"], t + 1)
                dve.wait_ge(x_sem[t % 4], 16 * (t // 4 + 1))
                dve.tensor_tensor(z[:, t, :], xin[:, t % 4, :], o[:, t, :], ALU.add).then_inc(s["x1"], 1)

        def sum_squares(pe, t):
            pe.wait_ge(s["sq"], t + 1)
            pe.matmul(bank[7][:], con(m, "ones"), sq[:, t % 2, :], start=t == 0, stop=t == KD - 1)\
              .then_inc(s["summed"], 1)

        @blk.tensor
        def _(pe):
            pe.sem_inc(s["unit_used"], 2)
            pe.wait_ge(s["y_lo"], KD)
            for t in range(KD):
                if t >= 2:
                    pe.wait_ge(s["copied"], t - 1)
                for j in range(2):
                    multiply_unit(pe, m, s, 2 * t + j, j, bank[t % 2][:], m["h_hi"], m["h_lo"], 8 * j, 8,
                                  j == 0, j == 1)
                if t:
                    sum_squares(pe, t - 1)
                if t % 4 == 0 and t:
                    g = t // 4 - 1
                    mod_columns(pe, m, s, bank[6], macc[:, g % 2, :], (MOD0 + g) * (GRP // P), KD * (g + 1) + NB)
            mod_columns(pe, m, s, bank[6], macc[:, (MG - 1) % 2, :], (MOD0 + MG - 1) * (GRP // P), KD * MG + NB)
            sum_squares(pe, KD - 1)


def stage_ffn(nc, mem, m, d, out):
    names = ("gate_at", "gate_c1", "gate_c2", "gelu", "val_at", "val_c1", "val_c2", "hid", "hid_hi", "hid_lo",
             "share", "zeroed", "sq", "summed", "root", "rstd", "normed", "x2", "stored")
    UU = 4
    NB, MOD0 = 2, 10
    MW = T
    GU = GT * UU + KD
    with nc.cleanup_on_exit(), ExitStack() as ctx:
        s = {n: nc.alloc_semaphore("ff_" + n) for n in names}
        s.update(ring_sems(nc, ctx, "ff"))
        s.update(mod_sems(nc, "ff", NB))
        x_sem = [nc.alloc_semaphore(f"ff_xin{j}") for j in range(4)]
        acc = m["z"]
        at = put_ring(mem, m, "ff_w", DUNIT)
        h_hi, at = mem.put("ff_hid_hi", [P, GT, T], F32R, at)
        h_lo, at = mem.put("ff_hid_lo", [P, GT, T], F32R, at)
        gate, at = mem.put("ff_gate", [P, T], F32, at)
        val, at = mem.put("ff_val", [P, T], F32, at)
        hid, at = mem.put("ff_hid", [P, T], F32, at)
        rstd, at = mem.put("ff_rstd", [P, T], F32, at)
        shared, at = mem.put("ff_shared", [P, NB + GROUPS, T], F32, at)
        mbuf, macc = shared[:, 0:NB, :], shared[:, NB:NB + GROUPS, :]
        xin = shared[:, 0:4, :]
        sq = (gate, val)
        bank = m["bank"]
        blk = ctx.enter_context(nc.Block())

        def conv(n, f):
            return vec(m, "conv", f + n * FT)

        @blk.sync
        def _(sp):
            with sp.Fori(0, GROUPS) as g:
                with sp.Fori(0, GT) as i:
                    for j in range(UU):
                        u = g * GU + i * UU + j
                        load_unit(sp, m, s, u, j % 2, g * (GU // 2) + i * 2 + (j // 2),
                                  row(d["w_up"], g * (GT * UU) + i * UU + j), UNIT)
                with sp.Fori(0, KD // 2) as t:
                    for j in range(2):
                        u = g * GU + t * 2 + (GT * UU + j)
                        load_unit(sp, m, s, u, j, g * (GU // 2) + t + (GT * 2), row(d["w_down"], g * KD + t * 2 + j),
                                  DUNIT)
                        load_mod(sp, s, mbuf, g * KD + t * 2 + j, j, row(d["w_mod_gate"], g * KD + t * 2 + j))
            sp.wait_ge(s["mod_cols"], GROUPS + 2)
            for t in range(KD):
                if t >= 4:
                    sp.wait_ge(s["x2"], t - 3)
                sp.dma_start(xin[:, t % 4, :], d["x1"][:, t, :]).then_inc(x_sem[t % 4], 16)
            for t in range(0, KD, 4):
                sp.wait_ge(s["x2"], t + 4)
                sp.dma_start(out[:, t:t + 4, :], acc[:, t:t + 4, :]).then_inc(s["stored"], 16)
            sp.wait_ge(s["stored"], 16 * (KD // 4))

        @blk.gpsimd
        def _(pool):
            pool.sem_inc(s["lo_ready"], 2)

            def tile(g, i, width):
                for j in range(2, 6):
                    remainder_unit(pool, m, s, g * GU + i * UU + j, j % 2, UNIT if j < 4 else width)
                pool.wait_ge(s["hid_hi"], g * GT + i + 1)
                pool.tensor_tensor(row(h_lo, i, 1), hid[:], row(h_hi, i, 1).bitcast(F32),
                                   ALU.subtract).then_inc(s["hid_lo"], 1)

            with pool.Fori(0, GROUPS) as g:
                for j in range(2):
                    remainder_unit(pool, m, s, g * GU + j, j, UNIT)
                with pool.Fori(0, GT - 1) as i:
                    tile(g, i, UNIT)
                tile(g, GT - 1, DUNIT)
                with pool.Fori(1, KD // 2) as t:
                    for j in range(2):
                        remainder_unit(pool, m, s, g * GU + t * 2 + (GT * UU + j), j, DUNIT)

        @blk.scalar
        def _(act):
            act.sem_inc(s["gelu"], 1)

            def tile(g, i, width):
                n = g * GT + i
                for j in (2, 3):
                    round_unit(act, m, s, g * GU + i * UU + j, j % 2, g * (GU // 2) + i * 2 + 1, UNIT)
                tile_done(act, s, g * GU + i * UU + 1)
                act.activation(gate[:], bank[0][:], ACT.Identity, scale=conv(2, n), bias=conv(3, n))\
                   .then_inc(s["gate_at"], 1)
                act.wait_ge(s["gate_c2"], n + 2)
                act.activation(gate[:], gate[:], ACT.Gelu_apprx_tanh).then_inc(s["gelu"], 1)
                for j in (4, 5):
                    round_unit(act, m, s, g * GU + i * UU + j, j % 2, g * (GU // 2) + i * 2 + 2, width)
                tile_done(act, s, g * GU + i * UU + 3)
                act.activation(val[:], bank[1][:], ACT.Identity, scale=conv(6, n), bias=conv(7, n))\
                   .then_inc(s["val_at"], 1)
                act.wait_ge(s["hid"], n + 1)
                act.activation(row(h_hi, i, 1), hid[:], ACT.Copy).then_inc(s["hid_hi"], 1)

            with act.Fori(0, GROUPS) as g:
                for j in range(2):
                    round_unit(act, m, s, g * GU + j, j, g * (GU // 2), UNIT)
                with act.Fori(0, GT - 1) as i:
                    tile(g, i, UNIT)
                tile(g, GT - 1, DUNIT)
                with act.Fori(1, KD // 2) as t:
                    for j in range(2):
                        round_unit(act, m, s, g * GU + t * 2 + (GT * UU + j), j, g * (GU // 2) + t + (GT * 2), DUNIT)
            for t in range(KD):
                if t >= 2:
                    act.wait_ge(s["summed"], t - 1)
                act.wait_ge(s["share"], (GROUPS - 1) * KD + t + 3)
                act.activation(sq[t % 2][:], acc[:, t, :], ACT.Square).then_inc(s["sq"], 1)
            act.wait_ge(s["summed"], KD)
            act.activation(rstd[:], bank[7][:], ACT.Sqrt, bias=m["eps"][:, 0:1], scale=1.0 / D).then_inc(s["root"], 1)

        @blk.vector
        def _(dve):
            dve.memset(acc[:], 0.0).then_inc(s["share"], 1)
            dve.sem_inc(s["share"], 1)
            dve.sem_inc(s["mod_summed"], NB - 1)
            dve.sem_inc(s["mod_cols"], 2)
            dve.memset(macc[:], 0.0).then_inc(s["mod_summed"], 1)
            with dve.Fori(0, GROUPS) as g:
                with dve.Fori(0, GT) as i:
                    n = g * GT + i
                    for tile, b, at, c1, c2, w in ((gate, 0, "gate_at", "gate_c1", "gate_c2", 0),
                                                   (val, 1, "val_at", "val_c1", "val_c2", 4)):
                        dve.wait_ge(s[at], n + 1)
                        dve.scalar_tensor_tensor(out=tile[:, 1:T], in0=bank[b][:, 0:T - 1], scalar=conv(w + 1, n),
                                                 in1=tile[:, 1:T], op0=ALU.mult, op1=ALU.add).then_inc(s[c1], 1)
                        dve.wait_ge(s[c1], n + 1)
                        dve.scalar_tensor_tensor(out=tile[:, 2:T], in0=bank[b][:, 0:T - 2], scalar=conv(w, n),
                                                 in1=tile[:, 2:T], op0=ALU.mult, op1=ALU.add).then_inc(s[c2], 1)
                    dve.wait_ge(s["val_c2"], n + 2)
                    dve.wait_ge(s["gelu"], n + 2)
                    dve.wait_ge(s["hid_lo"], n + 1)
                    dve.tensor_tensor(hid[:], gate[:], val[:], ALU.mult).then_inc(s["hid"], 1)
                with dve.Fori(0, KD // 2) as t:
                    for j in range(2):
                        add_mod(dve, m, s, mbuf, row(macc, g, 1), g * KD + t * 2 + j, j, g * (KD // 2) + t, NB, t * 2 + j)
                        tile_done(dve, s, g * GU + t * 2 + (GT * UU + j))
                        dve.wait_ge(s["share"], g * KD + t * 2 + (j + 2))
                        o = row(acc, t * 2 + j, 1)
                        dve.tensor_tensor(o, bank[2 + j][:], o, ALU.add).then_inc(s["share"], 1)
            finish_mod(dve, m, s, bank[4], 5 * KD, KD, GROUPS, (3, "g_post_ffn", 5 * KD))
            dve.wait_ge(s["root"], 1)
            dve.reciprocal(rstd[:], rstd[:]).then_inc(s["rstd"], 1)
            dve.wait_ge(s["rstd"], 1)
            for t in range(KD):
                dve.scalar_tensor_tensor(out=acc[:, t, :], in0=acc[:, t, :],
                                         scalar=m["gs"][:, 3 * KD + t:3 * KD + t + 1], in1=rstd[:],
                                         op0=ALU.mult, op1=ALU.mult).then_inc(s["normed"], 1)
                dve.wait_ge(s["normed"], t + 1)
                dve.wait_ge(x_sem[t % 4], 16 * (t // 4 + 1))
                dve.tensor_tensor(acc[:, t, :], xin[:, t % 4, :], acc[:, t, :], ALU.add).then_inc(s["x2"], 1)

        @blk.tensor
        def _(pe):
            pe.sem_inc(s["unit_used"], 2)
            pe.sem_inc(s["gate_c2"], 1)
            pe.sem_inc(s["val_c2"], 1)
            pe.sem_inc(s["hid_lo"], 1)
            with pe.Fori(0, GROUPS) as g:
                with pe.Fori(0, GT) as i:
                    n = g * GT + i
                    for b in range(2):
                        pe.wait_ge(s[("gate_c2", "val_c2")[b]], n + 1)
                        for j in (2 * b, 2 * b + 1):
                            multiply_unit(pe, m, s, g * GU + i * UU + j, j % 2, bank[b][:], m["h_hi"], m["h_lo"],
                                          8 * (j % 2), 8, j % 2 == 0, j % 2 == 1)
                with pe.Fori(0, KD // 2) as t:
                    pe.wait_ge(s["hid_lo"], g * GT + (GT + 1))
                    for j in range(2):
                        pe.wait_ge(s["share"], g * KD + t * 2 + (j + 1))
                        multiply_unit(pe, m, s, g * GU + t * 2 + (GT * UU + j), j, bank[2 + j][:], h_hi, h_lo,
                                      0, GT, True, True)
            for g in range(GROUPS):
                mod_columns(pe, m, s, bank[4], macc[:, g, :], 5 * KD + g * (MW // P), GROUPS * KD + NB)
            for t in range(KD):
                pe.wait_ge(s["sq"], t + 1)
                pe.matmul(bank[7][:], con(m, "ones"), sq[t % 2][:], start=t == 0, stop=t == KD - 1)\
                  .then_inc(s["summed"], 1)


def kernel(**inputs):
    from concourse import bacc
    from concourse.bass_utils import run_bass_kernel_spmd

    a = {n: np.asarray(v) for n, v in inputs.items()}

    def cols(v, pad=None):
        return np.ascontiguousarray(v.reshape(-1, P).T)

    def zeros(rows, width):
        return np.zeros((rows, width), np.float32)

    def units(w, kt):
        K, M = w.shape
        v = w.reshape(K // (kt * P), kt, P, M // P, P)
        return np.ascontiguousarray(v.transpose(3, 0, 2, 1, 4)).reshape(-1, P, kt * P)

    w = a["w_in"][0]
    lo = [3072, 3168, 3264, 3520, 4032, 4288, 4352]
    mu = a["mu_shift"][0]
    pad = zeros(D, 32)
    parts = [w[:, lo[2]:lo[3]], w[:, lo[0]:lo[1]], pad, w[:, lo[1]:lo[2]], pad]
    for p in range(NPAIR):
        parts += [w[:, g * 1024 + p * P:g * 1024 + (p + 1) * P] for g in range(3)]
    parts += [w[:, lo[3]:lo[5]], w[:, lo[5]:], w[:, lo[5]:]]
    w_in = units(np.concatenate(parts, 1), 8)
    z32 = np.zeros(32, np.float32)
    mu_cols = np.concatenate([mu[:3072], mu[lo[2]:lo[3]], mu[lo[0]:lo[1]], z32, mu[lo[1]:lo[2]], z32])
    cw, cb = a["conv_w"][0], a["conv_b"][0]
    conv = np.concatenate([np.concatenate([cw[0, h], cw[1, h], cw[2, h], cb[h]])
                           for h in (slice(0, FF), slice(FF, 2 * FF))])
    parts = [a["c"][0], a["b_mod"][0], a["g_pre_mix"][0], a["g_post_mix"][0], a["g_pre_ffn"][0], a["g_post_ffn"][0],
             mu_cols, a["w0"][0], a["a0"][0], a["k_k"][0], a["k_a"][0], a["r_k"][0].reshape(-1), a["ln_x_g"][0],
             a["ln_x_b"][0], a["q_norm_g"][0], a["kv_norm_g"][0], conv]
    vecs = cols(np.concatenate(parts))
    low = np.concatenate([a["w_gate_up"][0], a["w_decay_up"][0], zeros(32, 1024), a["w_iclr_up"][0], zeros(32, 1024)])
    low = np.ascontiguousarray(low.reshape(4, P, NPAIR, P).transpose(2, 1, 0, 3)).reshape(NPAIR, P, 4 * P)
    wq = a["w_q_up"][0].reshape(LATQ, P, 4, 2, NOPE + ROPE)
    wq = np.concatenate([wq[..., 0, :NOPE], wq[..., 1, :NOPE], wq[..., 0, NOPE:], wq[..., 1, NOPE:]], -1)
    wq = np.ascontiguousarray(wq.transpose(2, 1, 0, 3)).reshape(4, P, LATQ * 3 * P)
    wkv = a["w_kv_up"][0].reshape(LATKV, P, 4, 2, 2, P)
    wk, wv = (np.ascontiguousarray(wkv[:, :, :, :, n].transpose(2, 1, 0, 3, 4)).reshape(4, P, LATKV * 2 * P)
              for n in range(2))
    wm = a["w_mod"][0][:, :5 * D].reshape(KD, P, 5 * D // GRP, GRP)
    wm = np.ascontiguousarray(wm.transpose(2, 0, 1, 3)).reshape(-1, P, GRP)
    wg = a["w_mod"][0][:, 5 * D:].reshape(KD, P, GROUPS, D // GROUPS)
    wg = np.ascontiguousarray(wg.transpose(2, 0, 1, 3)).reshape(-1, P, D // GROUPS)
    up = a["w_ffn_up"][0].reshape(2, 8, P, 2, FT, P)
    up = np.ascontiguousarray(up.transpose(4, 3, 0, 2, 1, 5)).reshape(FT * 4, P, UNIT)
    dn = a["w_ffn_down"][0].reshape(GROUPS, GT, P, KD, P)
    dn = np.ascontiguousarray(dn.transpose(0, 3, 2, 1, 4)).reshape(GROUPS * KD, P, DUNIT)
    xt = np.ascontiguousarray(a["x"][0].T.reshape(KD, P, T).transpose(1, 0, 2))
    pos = np.ascontiguousarray(np.broadcast_to(a["positions"][0][None, :], (P, T)))

    arrays = {"vec": vecs, "con": constants(), "xt": xt, "pos": pos, "w_mod": wm, "w_mod_gate": wg, "w_in": w_in, "low": low,
              "w_q": wq, "w_k": wk, "w_v": wv, "w_out": units(a["w_out"][0], 8), "w_up": up, "w_down": dn}
    nc = bacc.Bacc("TRN2", target_bir_lowering=False, num_devices=1)
    d = {n: nc.dram_tensor("in_" + n, v.shape, mybir.dt.from_np(v.dtype), kind="ExternalInput").ap()
         for n, v in arrays.items()}
    d["x1"] = nc.dram_tensor("x1_kept", (P, KD, T), F32, kind="Internal").ap()
    out = nc.dram_tensor("out", (P, KD, T), F32, kind="ExternalOutput").ap()
    build_program(nc, d, out)
    r = run_bass_kernel_spmd(nc, [{"in_" + n: v for n, v in arrays.items()}], core_ids=[0])
    got = r.results[0]["out"]
    return np.ascontiguousarray(got.transpose(1, 0, 2).reshape(D, T).T).reshape(1, T, D)
```

```python
import math
from contextlib import ExitStack

import concourse.bass as bass
from concourse import mybir
import numpy as np

F32 = mybir.dt.float32
F32R = mybir.dt.float32r
I32 = mybir.dt.int32
ALU = mybir.AluOpType
ACT = mybir.ActivationFunctionType
AX_X = mybir.AxisListType.X

P = 128
D = 2048
T = 512
KD = D // P
CH = 64
NCH = T // CH
NPAIR = 8
LATQ, LATKV = 4, 2
NOPE, ROPE = 128, 64
SCALE = float(NOPE + ROPE) ** -0.5
FF = 5632
FT = FF // P
GROUPS = 4
GT = FT // GROUPS
UNIT = 8 * P
DUNIT = GT * P
NMOD = 6 * D // P
GRP = 1024
EPS = 1e-6
GN_EPS = 64e-5
DECAY_C = math.exp(-0.5)
LEVELS = [2, 4, 8, 16, 32]

VEC = {}
_at = 0
for _n, _w in (("c", 16), ("b_mod", 96), ("g_pre_mix", 16), ("g_post_mix", 16), ("g_pre_ffn", 16),
               ("g_post_ffn", 16), ("mu", 28), ("w0", 8), ("a0", 8), ("k_k", 8), ("k_a", 8),
               ("r_k", 8), ("ln_g", 8), ("ln_b", 8), ("q_g", 4), ("kv_g", 2), ("conv", 8 * FT)):
    VEC[_n] = _at
    _at += _w
NVEC = _at

CON = {}
_at = 0
for _n, _w in (("ident", P), ("ones", P), ("heads", P), ("below", CH), ("upto", CH), ("m1t", P), ("m1", P),
               ("m2", P), ("m4", P), ("m8", P), ("m16", P), ("m32", P), ("swap", P), ("early", P), ("late", P),
               ("reset", T), ("freq", 1)):
    CON[_n] = _at
    _at += _w
NCON = _at


def constants():
    con = np.zeros((P, NCON), np.float32)

    def put(name, a):
        con[:, CON[name]:CON[name] + a.shape[1]] = a

    i = np.arange(P)
    head = i[:, None] // CH == i[None, :] // CH
    put("ident", np.eye(P))
    put("ones", np.ones((P, P)))
    put("heads", head)
    j, t = (i % CH)[:, None], np.arange(CH)[None, :]
    put("below", j < t)
    put("upto", j <= t)
    for b in (1, 2, 4, 8, 16, 32):
        row, col = i[:, None], i[None, :]
        m = (row // (2 * b) == col // (2 * b)) & (row % (2 * b) >= b) & (col % (2 * b) < b)
        put(f"m{b}", m)
        if b == 1:
            put("m1t", m.T)
    swap = np.zeros((P, P))
    for m in range(P):
        h, r = m // ROPE * ROPE, m % ROPE
        if r < ROPE // 2:
            swap[h + r + ROPE // 2, m] = -1.0
        else:
            swap[h + r - ROPE // 2, m] = 1.0
    put("swap", swap)
    early = np.zeros((P, P))
    early[0, :CH] = 1.0
    late = np.zeros((P, P))
    late[0, CH:] = -1e30
    put("early", early)
    put("late", late)
    reset = np.ones((P, T))
    reset[:, ::CH] = 0.0
    put("reset", reset)
    freq = 10000.0 ** (-np.arange(0, ROPE, 2) / ROPE)
    put("freq", np.tile(freq.astype(np.float32), P // (ROPE // 2))[:, None])
    return con


class Mem:

    def __init__(self, nc):
        self.nc = nc
        at = (nc.sbuf_base + 63) // 64 * 64
        self.h = at
        self.z = self.h + 2 * KD * T * 4
        self.con = self.z + KD * T * 4
        self.ring = self.con + (NCON + NVEC + NMOD + 4 * KD + 28 + 8 + KD) * 4 + 7 * 64
        self.ring = (self.ring + 63) // 64 * 64
        self.work = self.ring + 6 * UNIT * 4
        self.end = nc.sbuf_usable_end
        self.whole = None

    def put(self, name, shape, dtype, offset):
        size = 4
        for n in shape[1:]:
            size *= n
        assert offset + size <= self.end, (name, offset + size - self.end)
        if dtype == F32 and offset >= self.work:
            if self.whole is None:
                self.whole = self.nc.alloc_sbuf_tensor_at("work", [P, (self.end - self.work) // 4], F32,
                                                          offset=self.work)
            start = (offset - self.work) // 4
            view = self.whole[:, start:start + size // 4]
            if len(shape) == 3:
                view = view.rearrange("p (a n) -> p a n", n=shape[2])
            if len(shape) == 4:
                view = view.rearrange("p (a b n) -> p a b n", b=shape[2], n=shape[3])
            return view, (offset + size + 63) // 64 * 64
        return self.nc.alloc_sbuf_tensor_at(name, shape, dtype, offset=offset), (offset + size + 63) // 64 * 64


def build_program(nc, d, out):
    with ExitStack() as ctx:
        mem = Mem(nc)
        m = {}
        m["h_hi"], at = mem.put("h_hi", [P, KD, T], F32R, mem.h)
        m["h_lo"], at = mem.put("h_lo", [P, KD, T], F32R, at)
        put_ring(mem, m, "w", UNIT)
        m["z"], at = mem.put("z", [P, KD, T], F32, mem.z)
        m["con"], at = mem.put("con", [P, NCON], F32, mem.con)
        m["vec"], at = mem.put("vec", [P, NVEC], F32, at)
        m["mod"], at = mem.put("mod", [P, NMOD], F32, at)
        m["gs"], at = mem.put("gs", [P, 4 * KD], F32, at)
        m["omm"], at = mem.put("omm", [P, 28], F32, at)
        m["eps"], at = mem.put("eps", [P, 8], F32, at)
        m["silu"], at = mem.put("silu", [P, KD], F32, at)
        rstd, at = mem.put("rstd", [P, T], F32, (mem.end - T * 4) // 64 * 64)
        m["rstd"] = rstd[:]
        m["bank"] = [ctx.enter_context(nc.psum_tensor(f"bank{b}", [P, T], F32)) for b in range(8)]
        stage_modulation(nc, mem, m, d)
        stage_rwkv(nc, mem, m, d)
        stage_attention(nc, mem, m, d)
        stage_mix_out(nc, mem, m, d)
        stage_ffn(nc, mem, m, d, out)


def put_ring(mem, m, name, width):
    m["w_raw"], at = mem.put(name + "_raw", [P, 2, width], F32, mem.ring)
    m["w_hi"], at = mem.put(name + "_hi", [P, 2, width], F32R, at)
    m["w_lo"], at = mem.put(name + "_lo", [P, 2, width], F32R, at)
    return at


def con(m, name, n=None):
    at = CON[name]
    return m["con"][:, at:at + (n or P)]


def vec(m, name, i=0):
    return m["vec"][:, bass.ds(i + VEC[name], 1)]


def row(ap, i, axis=0):
    if axis == 0:
        return ap[bass.ds(i, 1)].rearrange("a p n -> p (a n)")
    return ap[:, bass.ds(i, 1), :].rearrange("p a n -> p (a n)")


def over(ap, n):
    w = ap.shape[1]
    return ap.rearrange("p (a w) -> p a w", a=1).broadcast_to([ap.shape[0], n, w])



def ring_sems(nc, stage):
    s = {f"raw_loaded{j}": nc.alloc_semaphore(f"{stage}_raw_loaded{j}") for j in range(2)}
    for n in ("hi_ready", "lo_ready", "unit_used"):
        s[n] = nc.alloc_semaphore(f"{stage}_{n}")
    return s



def first_sems(nc, stage):
    return {n: nc.alloc_semaphore(f"{stage}_{n}") for n in ("first_loaded0", "first_loaded1", "first_hi")}


def load_first(sp, m, s, src):
    for j in range(2):
        sp.dma_start(m["w_raw"][:, j, :], src[j]).then_inc(s[f"first_loaded{j}"], 16)


def round_first(act, m, s):
    for j in range(2):
        act.wait_ge(s[f"first_loaded{j}"], 16)
        act.activation(m["w_hi"][:, j, :], m["w_raw"][:, j, :], ACT.Copy).then_inc(s["first_hi"], 1)


def remainder_first(pool, m, s):
    for j in range(2):
        pool.wait_ge(s["first_hi"], j + 1)
        pool.tensor_tensor(m["w_lo"][:, j, :], m["w_raw"][:, j, :], m["w_hi"][:, j, :].bitcast(F32), ALU.subtract)


def take_first(pool, s):
    pool.sem_inc(s["raw_loaded0"], 16)
    pool.sem_inc(s["raw_loaded1"], 16)
    pool.sem_inc(s["hi_ready"], 2)
    pool.sem_inc(s["lo_ready"], 4)


def load_unit(sp, m, s, u, slot, nth, src, width):
    sp.wait_ge(s["lo_ready"], u + 1)
    sp.dma_start(m["w_raw"][:, slot, 0:width], src).then_inc(s[f"raw_loaded{slot}"], 16)


def round_unit(act, m, s, u, slot, nth, width):
    act.wait_ge(s[f"raw_loaded{slot}"], (nth + 1) * 16)
    act.wait_ge(s["unit_used"], u + 1)
    act.activation(m["w_hi"][:, slot, 0:width], m["w_raw"][:, slot, 0:width], ACT.Copy).then_inc(s["hi_ready"], 1)


def remainder_unit(pool, m, s, u, slot, width):
    pool.wait_ge(s["hi_ready"], u + 1)
    pool.tensor_tensor(m["w_lo"][:, slot, 0:width], m["w_raw"][:, slot, 0:width],
                       m["w_hi"][:, slot, 0:width].bitcast(F32), ALU.subtract).then_inc(s["lo_ready"], 1)


def tile_done(eng, s, u):
    eng.wait_ge(s["unit_used"], u + 3)


def multiply_unit(pe, m, s, u, slot, bank, x_hi, x_lo, k0, n, first, last):
    multiply_part(pe, m, s, u, slot, bank, x_hi, x_lo, k0, 0, n, n, first, last)


def multiply_part(pe, m, s, u, slot, bank, x_hi, x_lo, k0, at, count, n, first, last):
    if at == 0:
        pe.wait_ge(s["lo_ready"], u + 3)
    for k in range(at, at + count):
        hi = m["w_hi"][:, slot, k * P:(k + 1) * P]
        lo = m["w_lo"][:, slot, k * P:(k + 1) * P]
        pe.matmul(bank, hi, x_hi[:, k0 + k, :], start=first and k == 0, stop=False)
        pe.matmul(bank, hi, x_lo[:, k0 + k, :], start=False, stop=False)
        mm = pe.matmul(bank, lo, x_hi[:, k0 + k, :], start=False, stop=last and k == n - 1)
    if at + count == n:
        mm.then_inc(s["unit_used"], 1)



def mod_sems(nc, stage, slots):
    s = {f"mod_landed{j}": nc.alloc_semaphore(f"{stage}_mod_landed{j}") for j in range(slots)}
    for n in ("mod_summed", "mod_cols", "mod_added"):
        s[n] = nc.alloc_semaphore(f"{stage}_{n}")
    return s


def load_mod(sp, s, buf, u, slot, src):
    sp.wait_ge(s["mod_summed"], u + 1)
    sp.dma_start(buf[:, slot, :], src).then_inc(s[f"mod_landed{slot}"], 16)


def add_mod(dve, m, s, buf, acc, u, slot, nth, slots, k, first=False):
    dve.wait_ge(s[f"mod_landed{slot}"], nth * 16 + 16)
    dve.wait_ge(s["mod_summed"], u + slots)
    column = m["silu"][:, bass.ds(k, 1)]
    if first:
        op = dve.tensor_scalar(acc, buf[:, slot, :], column, None, ALU.mult)
    else:
        op = dve.scalar_tensor_tensor(out=acc, in0=buf[:, slot, :], scalar=column, in1=acc, op0=ALU.mult, op1=ALU.add)
    op.then_inc(s["mod_summed"], 1)


def mod_columns(pe, m, s, bank, acc, c0, units):
    pe.wait_ge(s["mod_summed"], units)
    for q in range(acc.shape[1] // P):
        mm = pe.matmul(bank[:, c0 + q:c0 + q + 1], acc[:, q * P:(q + 1) * P], con(m, "ones", 1), start=True, stop=True)
    mm.then_inc(s["mod_cols"], 1)


def finish_mod(dve, m, s, bank, c0, n, groups, gain=None):
    dve.wait_ge(s["mod_cols"], groups + 2)
    dve.tensor_tensor(m["mod"][:, c0:c0 + n], bank[:, c0:c0 + n], m["vec"][:, VEC["b_mod"] + c0:VEC["b_mod"] + c0 + n],
                      ALU.add).then_inc(s["mod_added"], 1)
    which, g, col = gain
    dve.wait_ge(s["mod_added"], 1)
    dve.scalar_tensor_tensor(out=m["gs"][:, which * KD:(which + 1) * KD], in0=m["mod"][:, col:col + KD],
                             scalar=1.0 if which < 2 else 0.0, in1=m["vec"][:, VEC[g]:VEC[g] + KD],
                             op0=ALU.add, op1=ALU.mult).then_inc(s["mod_added"], 1)


def mod_unit(d, u):
    return row(d["w_mod"], u)


def two_pi_parts():
    left, parts = 2 * math.pi, []
    for _ in range(4):
        e = math.floor(math.log2(abs(left))) - 10
        part = math.floor(left / 2.0 ** e) * 2.0 ** e
        parts.append(part)
        left -= part
    parts[-1] += left
    return parts


def rotary_angles(dve, m, s, pos, ang, turns, rest):
    dve.tensor_copy(ang[:], pos[:]).then_inc(s["pos"], 1)
    dve.wait_ge(s["pos"], 1)
    dve.tensor_scalar(ang[:], ang[:], con(m, "freq", 1), None, ALU.mult).then_inc(s["ang"], 1)
    steps = [1]

    def step(op):
        steps[0] += 1
        op.then_inc(s["ang"], 1)
        dve.wait_ge(s["ang"], steps[0])

    def less(acc, part, e):
        step(dve.scalar_tensor_tensor(out=acc, in0=turns[:], scalar=-part * 2.0 ** e, in1=acc,
                                      op0=ALU.mult, op1=ALU.add))

    big = 1.5 * 2.0 ** 23
    parts = two_pi_parts()
    dve.wait_ge(s["ang"], 1)
    step(dve.memset(rest[:], 0.0))
    for e in (22, 11):
        step(dve.tensor_scalar(turns[:], ang[:], 1.0 / (2 * math.pi * 2 ** e), -0.5, ALU.mult, ALU.add))
        step(dve.tensor_scalar(turns[:], turns[:], big, None, ALU.add))
        step(dve.tensor_scalar(turns[:], turns[:], -big, None, ALU.add))
        for n, part in enumerate(parts):
            less(ang[:] if n < 2 else rest[:], part, e)
    step(dve.tensor_tensor(turns[:], ang[:], rest[:], ALU.add))
    step(dve.tensor_scalar(turns[:], turns[:], 1.0 / (2 * math.pi), big, ALU.mult, ALU.add))
    step(dve.tensor_scalar(turns[:], turns[:], -big, None, ALU.add))
    less(ang[:], parts[0], 0)
    less(ang[:], parts[1], 0)
    step(dve.tensor_tensor(ang[:], ang[:], rest[:], ALU.add))
    less(ang[:], parts[2], 0)
    less(ang[:], parts[3], 0)
    dve.tensor_scalar(ang[:], ang[:], float(np.float32(3.1415925)), -float(np.float32(3.1415925)),
                      ALU.min, ALU.max).then_inc(s["sin_in"], 1)
    dve.wait_ge(s["sin_in"], 1)
    dve.scalar_tensor_tensor(out=turns[:], in0=ang[:], scalar=-1.0, in1=ang[:], op0=ALU.mult,
                             op1=ALU.max).then_inc(s["sin_in"], 1)


def stage_modulation(nc, mem, m, d):
    NB = 16
    GROUPS_HERE = 4
    with nc.cleanup_on_exit(), ExitStack() as ctx:
        s = {n: nc.alloc_semaphore("mod_" + n) for n in ("loads", "first_loads", "silu", "squared", "summed", "root",
                                                     "pos", "ang", "sin_in", "sin_out", "kept")}
        s.update(mod_sems(nc, "mod", NB))
        s.update(first_sems(nc, "mod"))
        buf, _ = mem.put("mod_buf", [P, NB, GRP], F32, mem.h)
        acc, at = mem.put("mod_acc", [P, 2, GRP], F32, mem.work)
        pos, at = mem.put("mod_pos", [P, T], I32, at)
        ang, at = mem.put("mod_ang", [P, T], F32, at)
        turns, at = mem.put("mod_turns", [P, T], F32, at)
        rest, at = mem.put("mod_rest", [P, T], F32, at)
        tables, at = mem.put("mod_tables", [P, 2, T], F32, at)
        sq, at = mem.put("mod_sq", [P, 2, T], F32, at)
        sil = m["silu"]
        bank, sum_bank = m["bank"][0], m["bank"][1]
        blk = ctx.enter_context(nc.Block())

        @blk.sync
        def _(sp):
            sp.dma_start(m["con"][:], d["con"]).then_inc(s["first_loads"], 16)
            sp.dma_start(pos[:], d["pos"]).then_inc(s["first_loads"], 16)
            sp.dma_start(m["vec"][:], d["vec"]).then_inc(s["loads"], 16)
            sp.dma_start(m["z"][:], d["xt"]).then_inc(s["loads"], 16)
            with sp.Fori(0, GROUPS_HERE // 2) as i:
                for j in range(2 * KD):
                    load_mod(sp, s, buf, i * (2 * KD) + j, j % NB, mod_unit(d, i * (2 * KD) + j))
            load_first(sp, m, s, d["w_in"])
            sp.wait_ge(s["sin_out"], 2)
            sp.dma_start(d["tables"], tables[:]).then_inc(s["kept"], 16)
            sp.wait_ge(s["kept"], 16)

        @blk.scalar
        def _(act):
            act.wait_ge(s["loads"], 32)
            act.activation(sil[:], m["vec"][:, VEC["c"]:VEC["c"] + KD], ACT.Sigmoid).then_inc(s["silu"], 1)
            for k in range(KD):
                if k >= 2:
                    act.wait_ge(s["summed"], k - 1)
                act.activation(sq[:, k % 2, :], m["z"][:, k, :], ACT.Square).then_inc(s["squared"], 1)
            act.wait_ge(s["summed"], KD)
            act.wait_ge(s["silu"], 4)
            act.activation(m["rstd"], sum_bank[:], ACT.Sqrt, bias=m["eps"][:, 0:1], scale=1.0 / D)\
               .then_inc(s["root"], 1)
            act.wait_ge(s["sin_in"], 2)
            act.activation(tables[:, 1, :], ang[:], ACT.Sin).then_inc(s["sin_out"], 1)
            act.activation(tables[:, 0, :], turns[:], ACT.Sin, bias=m["eps"][:, 2:3], scale=-1.0)\
               .then_inc(s["sin_out"], 1)
            round_first(act, m, s)

        @blk.gpsimd
        def _(pool):
            remainder_first(pool, m, s)

        @blk.vector
        def _(dve):
            dve.sem_inc(s["mod_summed"], NB)
            dve.sem_inc(s["mod_cols"], 2)
            dve.memset(m["eps"][:, 0:1], EPS)
            dve.memset(m["eps"][:, 1:2], GN_EPS)
            dve.memset(m["eps"][:, 2:3], math.pi / 2).then_inc(s["silu"], 1)
            dve.wait_ge(s["first_loads"], 32)
            rotary_angles(dve, m, s, pos, ang, turns, rest)
            dve.wait_ge(s["silu"], 2)
            dve.tensor_tensor(sil[:], sil[:], m["vec"][:, VEC["c"]:VEC["c"] + KD], ALU.mult).then_inc(s["silu"], 1)
            dve.wait_ge(s["silu"], 3)
            dve.tensor_scalar(m["omm"][:], m["vec"][:, VEC["mu"]:VEC["mu"] + 28], -1.0, 1.0, ALU.mult, ALU.add)\
               .then_inc(s["silu"], 1)
            with dve.Fori(0, GROUPS_HERE // 2) as i:
                for j in range(2 * KD):
                    g, k = j // KD, j % KD
                    if k == 0:
                        dve.wait_ge(s["mod_cols"], i * 2 + (g + 1))
                    add_mod(dve, m, s, buf, acc[:, g, :], i * (2 * KD) + j, j % NB, i * (2 * KD // NB) + j // NB, NB,
                            k, k == 0)
            dve.wait_ge(s["root"], 1)
            dve.reciprocal(m["rstd"], m["rstd"])
            finish_mod(dve, m, s, bank, 0, 2 * KD, GROUPS_HERE, (0, "g_pre_mix", KD))

        @blk.tensor
        def _(pe):
            pe.wait_ge(s["first_loads"], 32)
            for k in range(KD):
                pe.wait_ge(s["squared"], k + 1)
                pe.matmul(sum_bank[:], con(m, "ones"), sq[:, k % 2, :], start=k == 0, stop=k == KD - 1)\
                  .then_inc(s["summed"], 1)
            for g in range(GROUPS_HERE):
                mod_columns(pe, m, s, bank, acc[:, g % 2, :], g * (GRP // P), KD * (g + 1) + NB)



def h_sems(nc, stage):
    names = ("h_scaled", "h_rounded", "h_shifted_act", "h_shifted_dve", "h_lo_pool", "h_lo_dve")
    return {n: nc.alloc_semaphore(f"{stage}_{n}") for n in names}


def wait_shifted(eng, s, k):
    eng.wait_ge(s[("h_shifted_act", "h_shifted_dve")[k % 2]], k // 2 + 1)


def wait_h(eng, s, k):
    eng.wait_ge(s["h_lo_pool"], k + 1 - (k + 1) // 4)
    if k >= 3:
        eng.wait_ge(s["h_lo_dve"], (k + 1) // 4)


def h_on_act(act, m, s, tmp, first_mod, between):
    for k in range(KD):
        if k in between:
            between[k]()
        if k % 2 == 0:
            act.wait_ge(s["h_scaled"], k + 1)
            act.activation(tmp[:, k % 4, :], tmp[:, k % 4, :], ACT.Identity,
                           bias=m["mod"][:, first_mod + k:first_mod + k + 1]).then_inc(s["h_shifted_act"], 1)
        wait_shifted(act, s, k)
        act.activation(m["h_hi"][:, k, :], tmp[:, k % 4, :], ACT.Copy).then_inc(s["h_rounded"], 1)


def h_on_dve(dve, m, s, tmp, half, first_mod):
    def low(k):
        dve.wait_ge(s["h_rounded"], k + 1)
        dve.tensor_tensor(m["h_lo"][:, k, :], tmp[:, k % 4, :], m["h_hi"][:, k, :].bitcast(F32),
                          ALU.subtract).then_inc(s["h_lo_dve"], 1)

    for k in range(KD):
        if k >= 4:
            if k % 4 == 3:
                dve.wait_ge(s["h_lo_dve"], k // 4)
            else:
                dve.wait_ge(s["h_lo_pool"], k - 3 - (k - 3) // 4)
        dve.scalar_tensor_tensor(out=tmp[:, k % 4, :], in0=m["z"][:, k, :],
                                 scalar=m["gs"][:, half * KD + k:half * KD + k + 1], in1=m["rstd"],
                                 op0=ALU.mult, op1=ALU.mult).then_inc(s["h_scaled"], 1)
        if k % 2:
            c0 = first_mod + k
            dve.wait_ge(s["h_scaled"], k + 1)
            dve.tensor_scalar(tmp[:, k % 4, :], tmp[:, k % 4, :], m["mod"][:, c0:c0 + 1], None,
                              ALU.add).then_inc(s["h_shifted_dve"], 1)
        if k % 4 == 1 and k > 1:
            low(k - 2)
    low(KD - 1)


def h_on_pool(pool, m, s, tmp, between):
    for k in range(KD):
        if k in between:
            between[k]()
        if k % 4 < 3:
            pool.wait_ge(s["h_rounded"], k + 1)
            pool.tensor_tensor(m["h_lo"][:, k, :], tmp[:, k % 4, :], m["h_hi"][:, k, :].bitcast(F32),
                               ALU.subtract).then_inc(s["h_lo_pool"], 1)


def multiply_first(pe, m, s, u, slot, bank, k0, first, last):
    for k in range(0, 8, 2):
        wait_h(pe, s, k0 + k + 1)
        multiply_part(pe, m, s, u, slot, bank, m["h_hi"], m["h_lo"], k0, k, 2, 8, first, last)


def stage_rwkv(nc, mem, m, d):
    NU, PU = 8, 6
    NL = len(LEVELS)
    names = ("low_scaled", "low_shifted", "low_ready", "up_loaded", "up_done", "gates_read",
             "scaled", "shifted", "kk_raw", "kk_sq", "ss_sum", "ss_max", "norm", "norm_inv", "kk",
             "scan", "scan_x", "e_in", "e_ex", "e_inv", "kfac", "k2", "rk", "rk_sum", "bonus", "b", "rt", "at",
             "kbd", "bbd", "abd", "vbd", "tr_done", "tr_read", "prod_done", "ab", "ak", "rb", "rk_t",
             "amat", "x1", "x0", "xt0", "xt1", "tp", "t", "xp", "x", "xt", "wp", "w", "up", "u", "sd", "sp", "s",
             "yp", "y", "mean", "dev", "dev_sq", "var", "gstd", "grstd", "yn", "ya", "yb", "pair_done", "zeroed",
             "dc")
    with nc.cleanup_on_exit(), ExitStack() as ctx:
        s = {n: nc.alloc_semaphore("rw_" + n) for n in names}
        s.update(ring_sems(nc, "rw"))
        s.update(h_sems(nc, "rw"))
        z = m["z"]
        r, k, v, sw, L, a, kk, t1 = (z[:, 8 + n, :] for n in range(8))
        lat3, at = mem.put("rw_lat", [P, 3, T], F32, mem.work)
        lat = [lat3[:, n, :] for n in range(3)] + [z[:, NPAIR - 2, :]]
        low = z[:, NPAIR - 1, :].rearrange("p (a n) -> p a n", a=4)
        t2, at = mem.put("rw_t2", [P, T], F32, at)
        ARs, at = mem.put("rw_AR", [P, 2, NCH * 2, CH], F32, at)
        Abds, at = mem.put("rw_Abd", [P, 2, NCH, P], F32, at)
        gs, at = mem.put("rw_g", [P, 2, T], F32, at)
        bonus, at = mem.put("rw_bonus", [P, 2, T], F32, at)
        dCs, at = mem.put("rw_dC", [P, 2, NCH], F32, at)
        Kbd, at = mem.put("rw_Kbd", [P, NCH, P], F32, at)
        Bbd, at = mem.put("rw_Bbd", [P, NCH, P], F32, at)
        Vbd, at = mem.put("rw_Vbd", [P, NCH, P], F32, at)
        XT, at = mem.put("rw_XT", [P, NCH, P], F32, at)
        Kt, at = mem.put("rw_Kt", [P, NCH, P], F32, at)
        Bt, at = mem.put("rw_Bt", [P, NCH, P], F32, at)
        Vt, at = mem.put("rw_Vt", [P, NCH, P], F32, at)
        AbT, at = mem.put("rw_AbT", [P, NCH, P], F32, at)
        AkT, at = mem.put("rw_AkT", [P, NCH, P], F32, at)
        RbT, at = mem.put("rw_RbT", [P, NCH, CH], F32, at)
        RkT, at = mem.put("rw_RkT", [P, NCH, CH], F32, at)
        S, at = mem.put("rw_S", [P, 2, P], F32, at)
        Sd, at = mem.put("rw_Sd", [P, P], F32, at)
        W, at = mem.put("rw_W", [P, P], F32, at)
        U, at = mem.put("rw_U", [P, P], F32, at)
        tmp = ARs.rearrange("p q x t -> p (q x t)").rearrange("p (a n) -> p a n", n=T)
        X, TT = Kbd, Vbd
        bank = m["bank"]
        prj = bank[0:3]
        chain, ybank = bank[3], bank[7]
        wcol, ucol, scol = (chain[:, n * P:(n + 1) * P] for n in range(3))
        HALF = (slice(0, CH), slice(CH, P))
        EARLY = [2, 2, 4]
        SHARE = [3] + [0, 1] * 2 + [1] * 17 + [3] + [1] * 11 + [2, 2]
        LAST_SHARE = [1] * 10 + [2] * 24 + [3] * 2
        assert sum(EARLY) == 8 and sum(SHARE) == 8 * (PU - 1) and sum(LAST_SHARE) == 8 * (PU + 2)

        def rounded_in(share, c, units):
            def used(n):
                return sum(share[:12 + 3 * n] if n >= 0 else share[:9]) // 8

            return [j for j in range(1, units) if j - 1 <= used(c) and (c < 0 or j - 1 > used(c - 1))]

        blk = ctx.enter_context(nc.Block())

        def chunks(ap):
            return ap.rearrange("p (c t) -> p c t", t=CH)

        def four(b):
            return b[:].rearrange("p (c t) -> p c t", t=P)

        def AR(q):
            return ARs[:, q, :, :].rearrange("p (c x) t -> p c x t", x=2)

        def in_turn(eng, pair):
            with eng.Fori(0, NPAIR // 2 - 1) as i:
                for q in range(2):
                    pair(i * 2 + q, q, True)
            pair(NPAIR - 2, 0, True)
            pair(NPAIR - 1, 1, False)

        @blk.sync
        def _(sp):
            def load_pair(p):
                for j in range(PU):
                    load_unit(sp, m, s, p * PU + (NU + j), j % 2, p * (PU // 2) + (NU // 2 + j // 2),
                              row(d["w_in"], p * PU + (NU + j)), UNIT)

            def load_low(p):
                sp.wait_ge(s["up_done"], p + 1)
                sp.dma_start(low, row(d["low"], p).rearrange("p (a n) -> p a n", a=4)).then_inc(s["up_loaded"], 16)

            for u in range(2, NU):
                load_unit(sp, m, s, u, u % 2, u // 2, d["w_in"][u], UNIT)
            wait_h(sp, s, KD - 1)
            load_low(0)
            load_pair(0)
            load_pair(1)

            def pair(p, q, ahead):
                if ahead:
                    load_low(p + 1)
                load_pair(p + 2)

            in_turn(sp, pair)
            for j in range(2):
                u = (NPAIR + 2) * PU + NU + j
                load_unit(sp, m, s, u, j, u // 2, d["w_in"][u], UNIT)

        @blk.gpsimd
        def _(pool):
            take_first(pool, s)
            h_on_pool(pool, m, s, tmp, {})
            for u in range(2, NU + 2 * PU):
                remainder_unit(pool, m, s, u, u % 2, UNIT)
                if 3 < u < 10:
                    tile = (Abds, Kbd, Bbd, Vbd, AbT, AkT)[u - 4]
                    pool.memset(tile[:], 0.0).then_inc(s["zeroed"], 1)
            with pool.Fori(2, NPAIR + 2) as p:
                for j in range(PU):
                    remainder_unit(pool, m, s, p * PU + (NU + j), j % 2, UNIT)
            for j in range(2):
                remainder_unit(pool, m, s, (NPAIR + 2) * PU + (NU + j), j, UNIT)

        @blk.scalar
        def _(act):
            def round_pair(p, j):
                round_unit(act, m, s, p * PU + (NU + j), j % 2, p * (PU // 2) + (NU // 2 + j // 2), UNIT)

            def unshifted(p, rounded=True):
                for n, dst in enumerate((r, k, v)):
                    if n == 2 and rounded:
                        round_pair(p + 1, 0)
                    tile_done(act, s, p * PU + (NU + 2 * n + 1))
                    act.activation(dst, prj[n][:], ACT.Identity,
                                   scale=m["omm"][:, bass.ds(p + 8 * n, 1)]).then_inc(s["scaled"], 1)

            def latent(p, n, dst):
                tile_done(act, s, p * PU + (NU + 2 * n + 1))
                act.activation(dst, bank[n if n < 3 else 4][:], ACT.Copy).then_inc(s["shifted"], 1)

            def prepare(p, q, part):
                if part == 0:
                    act.wait_ge(s["up_done"], p + 2)
                    act.activation(sw, bank[4][:], ACT.Sigmoid, bias=vec(m, "w0", p)).then_inc(s["gates_read"], 1)
                    act.activation(a, bank[5][:], ACT.Sigmoid, bias=vec(m, "a0", p)).then_inc(s["gates_read"], 1)
                    act.activation(gs[:, q, :], bank[6][:], ACT.Copy).then_inc(s["gates_read"], 1)
                if part == 1:
                    act.wait_ge(s["kk_raw"], p + 1)
                    act.activation(t2[:], kk, ACT.Square).then_inc(s["kk_sq"], 1)
                if part == 2:
                    act.wait_ge(s["scan_x"], p + 1)
                    act.activation(sw, L, ACT.Exp, scale=-DECAY_C).then_inc(s["e_in"], 1)
                    act.activation(t1, t1, ACT.Exp, scale=-DECAY_C).then_inc(s["e_ex"], 1)
                if part == 3:
                    act.wait_ge(s["e_in"], p + 1)
                    act.activation(L, L, ACT.Exp, scale=DECAY_C).then_inc(s["e_inv"], 1)
                    act.activation(dCs[:, q, :], chunks(sw)[:, :, CH - 1], ACT.Copy).then_inc(s["dc"], 1)
                    act.wait_ge(s["ss_max"], p + 1)
                    act.activation(t2[:], t2[:], ACT.Sqrt).then_inc(s["norm"], 1)
                if part == 5:
                    act.wait_ge(s["shifted"], p * 3 + 3)
                    for h in HALF:
                        act.activation(Vbd[h, :, h], chunks(v)[h], ACT.Copy).then_inc(s["vbd"], 1)
                if part == 7:
                    act.wait_ge(s["at"], p + 1)
                    for h in HALF:
                        act.activation(Abds[h, q, :, h], AR(q)[h, :, 0, :], ACT.Copy).then_inc(s["abd"], 1)

            def low_unshifted(t):
                tile_done(act, s, 2 * t + 1)
                act.activation(lat[t], bank[t][:], ACT.Identity,
                               scale=m["omm"][:, 24 + t:25 + t]).then_inc(s["low_scaled"], 1)

            h_on_act(act, m, s, tmp, 0, {})
            for u in range(NU):
                if u > 1:
                    round_unit(act, m, s, u, u % 2, u // 2, UNIT)
                if u % 2 == 1 and u > 1:
                    low_unshifted(u // 2 - 1)
            for j in range(2):
                round_pair(0, j)
            low_unshifted(3)
            for t, f in enumerate((ACT.Sigmoid, ACT.Sigmoid, ACT.Tanh)):
                act.wait_ge(s["low_shifted"], t + 1)
                act.activation(lat[t], lat[t], f).then_inc(s["low_ready"], 1)
            act.wait_ge(s["zeroed"], 6)
            for j in range(2, PU):
                round_pair(0, j)
            unshifted(0, False)
            for part in range(8):
                if part < PU:
                    round_pair(1, part)
                prepare(0, 0, part)

            def pair(p, q, ahead):
                for n, dst in enumerate((Kt, Bt, Vt)):
                    for o in range(2):
                        act.wait_ge(s["tr_done"], p * 6 + (2 * n + o + 1))
                        act.activation(dst[:, 4 * o:4 * o + 4, :], four(bank[3 + (2 * n + o) % 4]),
                                       ACT.Copy).then_inc(s["tr_read"], 1)
                if ahead:
                    unshifted(p + 1)
                else:
                    for n, dst in enumerate((r, k, v)):
                        if n == 2:
                            round_pair(p + 2, 0)
                        latent(p + 1, n, dst)
                share, units = (SHARE, PU) if ahead else (LAST_SHARE, PU + 2)
                assert sum(len(rounded_in(share, c, units)) for c in range(-1, NCH)) == units - 1
                for j in rounded_in(share, -1, units):
                    round_pair(p + 2, j)
                for c in range(NCH):
                    act.wait_ge(s["wp"], p * NCH + (c + 1))
                    act.activation(W[:], wcol, ACT.Copy).then_inc(s["w"], 1)
                    if c:
                        act.wait_ge(s["s"], p * NCH + c)
                        act.activation(Sd[:], S[:, c % 2, :], ACT.Copy, scale=dCs[:, q, c:c + 1]).then_inc(s["sd"], 1)
                    act.wait_ge(s["up"], p * NCH + (c + 1))
                    act.activation(U[:], ucol, ACT.Copy).then_inc(s["u"], 1)
                    for j in rounded_in(share, c, units):
                        round_pair(p + 2, j)
                    if not ahead and c in (3, 5, 7):
                        latent(p + 2, (c - 3) // 2, (sw, L, a)[(c - 3) // 2])
                    if ahead:
                        prepare(p + 1, 1 - q, c)
                act.wait_ge(s["yp"], p * NCH + NCH)
                act.activation(row(z, p, 1), ybank[:], ACT.Copy).then_inc(s["y"], 1)
                act.wait_ge(s["dev"], p + 1)
                act.activation(t1, t2[:], ACT.Square).then_inc(s["dev_sq"], 1)
                act.wait_ge(s["var"], p + 1)
                act.activation(t1, ybank[:], ACT.Sqrt, bias=m["eps"][:, 1:2], scale=1.0 / CH).then_inc(s["gstd"], 1)

            in_turn(act, pair)
            latent(NPAIR + 1, 3, kk)

        @blk.vector
        def _(dve):
            def shift(p):
                for n, dst in enumerate((r, k, v)):
                    dve.wait_ge(s["scaled"], p * 3 + (n + 1))
                    dve.scalar_tensor_tensor(out=dst[:, 1:T], in0=prj[n][:, 0:T - 1], scalar=vec(m, "mu", p + 8 * n),
                                             in1=dst[:, 1:T], op0=ALU.mult, op1=ALU.add).then_inc(s["shifted"], 1)

            def prepare(p, q, part):
                def after(name, i=0, n=1):
                    dve.wait_ge(s[name], p * n + (i + 1))

                if part == 0:
                    after("shifted", 1, 3)
                    dve.tensor_scalar(kk, k, vec(m, "k_k", p), None, ALU.mult).then_inc(s["kk_raw"], 1)
                if part == 1:
                    after("gates_read", 2, 3)
                    dve.tensor_tensor_scan(L, con(m, "reset", T), sw, 0.0, ALU.mult, ALU.add).then_inc(s["scan"], 1)
                    after("scan")
                    dve.tensor_tensor(t1, L, sw, ALU.subtract).then_inc(s["scan_x"], 1)
                if part == 2:
                    after("ss_sum")
                    dve.tensor_scalar(t2[:], bank[4][:], 1e-24, None, ALU.max).then_inc(s["ss_max"], 1)
                if part == 3:
                    after("norm")
                    dve.reciprocal(t2[:], t2[:]).then_inc(s["norm_inv"], 1)
                if part == 4:
                    after("norm_inv")
                    dve.tensor_tensor(kk, kk, t2[:], ALU.mult).then_inc(s["kk"], 1)
                    after("kk")
                    dve.tensor_scalar(t2[:], a, -1.0, vec(m, "k_a", p), ALU.add, ALU.mult).then_inc(s["kfac"], 1)
                    after("kfac")
                    dve.scalar_tensor_tensor(out=k, in0=t2[:], scalar=1.0, in1=k, op0=ALU.add,
                                             op1=ALU.mult).then_inc(s["k2"], 1)
                if part == 5:
                    after("k2")
                    dve.scalar_tensor_tensor(out=t2[:], in0=r, scalar=vec(m, "r_k", p), in1=k,
                                             op0=ALU.mult, op1=ALU.mult).then_inc(s["rk"], 1)
                    dve.tensor_tensor(a, kk, a, ALU.mult).then_inc(s["b"], 1)
                    after("e_in")
                    dve.tensor_tensor(AR(q)[:, :, 1, :], chunks(r), chunks(sw), ALU.mult).then_inc(s["rt"], 1)
                if part == 6:
                    after("e_ex")
                    dve.scalar_tensor_tensor(out=AR(q)[:, :, 0, :], in0=chunks(kk), scalar=-1.0, in1=chunks(t1),
                                             op0=ALU.mult, op1=ALU.mult).then_inc(s["at"], 1)
                    after("e_inv")
                    after("b")
                    for h in HALF:
                        dve.tensor_tensor(Kbd[h, :, h], chunks(k)[h], chunks(L)[h], ALU.mult).then_inc(s["kbd"], 1)
                if part == 7:
                    after("rk_sum")
                    dve.tensor_tensor(bonus[:, q, :], bank[5][:], v, ALU.mult).then_inc(s["bonus"], 1)
                    for h in HALF:
                        dve.tensor_tensor(Bbd[h, :, h], chunks(a)[h], chunks(L)[h], ALU.mult).then_inc(s["bbd"], 1)

            h_on_dve(dve, m, s, tmp, 0, 0)
            for t in range(4):
                dve.wait_ge(s["low_scaled"], t + 1)
                dve.scalar_tensor_tensor(out=lat[t][:, 1:T], in0=bank[t][:, 0:T - 1], scalar=vec(m, "mu", 24 + t),
                                         in1=lat[t][:, 1:T], op0=ALU.mult, op1=ALU.add).then_inc(s["low_shifted"], 1)
            dve.wait_ge(s["zeroed"], 6)
            shift(0)
            for part in range(8):
                prepare(0, 0, part)

            def pair(p, q, ahead):
                def after(name, i=0, n=1):
                    dve.wait_ge(s[name], p * n + (i + 1))

                for o in range(4):
                    after("prod_done", o, 4)
                    pr = bank[3 + o][:].rearrange("p (c x t) -> p c x t", c=2, x=4)
                    cc = slice(2 * o, 2 * o + 2)
                    for h in HALF:
                        dve.tensor_tensor(AbT[h, cc, h], pr[h, :, 0, :], over(con(m, "below", CH)[h], 2),
                                          ALU.mult).then_inc(s["ab"], 1)
                    for h in HALF:
                        dve.tensor_tensor(AkT[h, cc, h], pr[h, :, 2, :], over(con(m, "below", CH)[h], 2),
                                          ALU.mult).then_inc(s["ak"], 1)
                    dve.tensor_tensor(RbT[:, cc, :], pr[:, :, 1, :], over(con(m, "upto", CH), 2),
                                      ALU.mult).then_inc(s["rb"], 1)
                    dve.tensor_tensor(RkT[:, cc, :], pr[:, :, 3, :], over(con(m, "upto", CH), 2),
                                      ALU.mult).then_inc(s["rk_t"], 1)
                after("ab", 7, 8)
                dve.tensor_tensor(XT[:], AbT[:], over(con(m, "m1t"), NCH), ALU.mult).then_inc(s["xt0"], 1)
                for o in range(2):
                    cc = slice(4 * o, 4 * o + 4)
                    after("amat", o, 2)
                    dve.tensor_tensor(X[:, cc, :], four(bank[3 + 2 * o]), over(con(m, "m1"), 4),
                                      ALU.mult).then_inc(s["x0"], 1)
                    after("x0", o, 2)
                    dve.tensor_tensor(X[:, cc, :], X[:, cc, :], over(con(m, "ident"), 4),
                                      ALU.add).then_inc(s["x1"], 1)
                after("xt0")
                dve.tensor_tensor(XT[:], XT[:], over(con(m, "ident"), NCH), ALU.add).then_inc(s["xt1"], 1)
                if ahead:
                    shift(p + 1)
                for l, b in enumerate(LEVELS):
                    for o in range(2):
                        after("tp", 2 * l + o, 2 * NL)
                        dve.tensor_tensor(TT[:, 4 * o:4 * o + 4, :], four(bank[3 + 2 * o]), over(con(m, f"m{b}"), 4),
                                          ALU.mult).then_inc(s["t"], 1)
                    for o in range(2):
                        cc = slice(4 * o, 4 * o + 4)
                        after("xp", 2 * l + o, 2 * NL)
                        if l:
                            after("xt", 2 * (l - 1) + o, 2 * NL)
                        if l < NL - 1:
                            dve.tensor_tensor(X[:, cc, :], four(bank[3 + 2 * o]), X[:, cc, :],
                                              ALU.add).then_inc(s["x"], 1)
                        dve.tensor_tensor(XT[:, cc, :], four(bank[4 + 2 * o]), XT[:, cc, :],
                                          ALU.add).then_inc(s["xt"], 1)
                for c in range(NCH):
                    after("sp", c, NCH)
                    if c:
                        after("yp", c - 1, NCH)
                        after("sd", c - 1, NCH - 1)
                        dve.scalar_tensor_tensor(out=S[:, (c + 1) % 2, :], in0=scol, scalar=dCs[:, q, c:c + 1],
                                                 in1=Sd[:], op0=ALU.mult, op1=ALU.add).then_inc(s["s"], 1)
                    else:
                        after("dc")
                        dve.tensor_scalar(S[:, 1, :], scol, dCs[:, q, 0:1], None, ALU.mult).then_inc(s["s"], 1)
                    if ahead:
                        prepare(p + 1, 1 - q, c)
                zp = row(z, p, 1)
                after("mean")
                dve.scalar_tensor_tensor(out=t2[:], in0=ybank[:], scalar=-1.0 / CH, in1=zp, op0=ALU.mult,
                                         op1=ALU.add).then_inc(s["dev"], 1)
                after("gstd")
                dve.reciprocal(t1, t1).then_inc(s["grstd"], 1)
                after("grstd")
                dve.tensor_tensor(t2[:], t2[:], t1, ALU.mult).then_inc(s["yn"], 1)
                after("yn")
                dve.tensor_scalar(t2[:], t2[:], vec(m, "ln_g", p), vec(m, "ln_b", p), ALU.mult,
                                  ALU.add).then_inc(s["ya"], 1)
                after("ya")
                dve.tensor_tensor(t2[:], t2[:], bonus[:, q, :], ALU.add).then_inc(s["yb"], 1)
                after("yb")
                dve.tensor_tensor(zp, t2[:], gs[:, q, :], ALU.mult).then_inc(s["pair_done"], 1)

            in_turn(dve, pair)

        @blk.tensor
        def _(pe):
            def project(p, j):
                multiply_unit(pe, m, s, p * PU + (NU + j), j % 2, prj[j // 2][:], m["h_hi"], m["h_lo"], 8 * (j % 2), 8,
                              j % 2 == 0, j % 2 == 1)

            def fill(p, gap, share):
                first = 8 * (PU - 1) if share is EARLY else 0
                for kt in range(first + sum(share[:gap]), first + sum(share[:gap + 1])):
                    j = kt // 8
                    if kt % 16 == 0 and j < PU:
                        pe.wait_ge(s["shifted"], p * 3 + (j // 2 - 2))
                    b = prj[j // 2] if j < PU else bank[4]
                    multiply_part(pe, m, s, p * PU + (NU + j), j % 2, b[:], m["h_hi"], m["h_lo"],
                                  8 * (j % 2), kt % 8, 1, 8, j % 2 == 0, j % 2 == 1)

            def prepare(p, part):
                if part == 0:
                    pe.wait_ge(s["up_loaded"], p * 16 + 16)
                    pe.matmul(bank[4][:], low[:, 2, :], lat[2], start=True, stop=True)
                    pe.matmul(bank[5][:], low[:, 3, :], lat[3], start=True, stop=True)
                    pe.matmul(bank[6][:], low[:, 0, :], lat[0], start=True, stop=False)
                    pe.matmul(bank[6][:], low[:, 1, :], lat[1], start=False, stop=True).then_inc(s["up_done"], 1)
                if part == 2:
                    pe.wait_ge(s["kk_sq"], p + 1)
                    pe.matmul(bank[4][:], con(m, "heads"), t2[:], start=True, stop=True).then_inc(s["ss_sum"], 1)
                if part == 6:
                    pe.wait_ge(s["rk"], p + 1)
                    pe.matmul(bank[5][:], con(m, "heads"), t2[:], start=True, stop=True).then_inc(s["rk_sum"], 1)

            pe.sem_inc(s["unit_used"], 2)
            pe.sem_inc(s["up_done"], 1)
            for u in range(2):
                multiply_first(pe, m, s, u, u, bank[0][:], 8 * u, u == 0, u == 1)
            for u in range(2, NU):
                multiply_unit(pe, m, s, u, u % 2, bank[u // 2][:], m["h_hi"], m["h_lo"], 8 * (u % 2), 8,
                              u % 2 == 0, u % 2 == 1)
            pe.wait_ge(s["low_shifted"], 4)
            for j in range(PU):
                project(0, j)
            pe.wait_ge(s["low_ready"], 3)
            for part in range(8):
                prepare(0, part)
                if part < PU - 1:
                    if part % 2 == 0:
                        pe.wait_ge(s["shifted"], part // 2 + 1)
                    project(1, part)

            def pair(p, q, ahead):
                def after(name, i=0, n=1):
                    pe.wait_ge(s[name], p * n + (i + 1))

                def each(lhsT, rhs, b, o):
                    for n in range(4):
                        mm = pe.matmul(bank[b][:, n * P:(n + 1) * P], lhsT[:, 4 * o + n, :], rhs(4 * o + n),
                                       start=True, stop=True)
                    return mm

                share = SHARE if ahead else LAST_SHARE
                for n, (tile, name) in enumerate(((Kbd, "kbd"), (Bbd, "bbd"), (Vbd, "vbd"))):
                    after(name, 1, 2)
                    for o in range(2):
                        if 2 * n + o == 2:
                            after("bonus")
                        if 2 * n + o >= 4:
                            after("tr_read", 2 * n + o - 4, 6)
                        for i in range(4):
                            mm = pe.transpose(bank[3 + (2 * n + o) % 4][:, i * P:(i + 1) * P], tile[:, 4 * o + i, :],
                                              con(m, "ident"))
                        mm.then_inc(s["tr_done"], 1)
                after("rt")
                after("at")
                for o in range(4):
                    after("tr_read", o + 2 if o > 1 else o + 4, 6)
                    for c in (2 * o, 2 * o + 1):
                        w = (c % 2) * 2 * P
                        ar = AR(q)[:, c, :, :].rearrange("p x t -> p (x t)")
                        pe.matmul(bank[3 + o][:, w:w + P], Bbd[:, c, :], ar, start=True, stop=True)
                        mm = pe.matmul(bank[3 + o][:, w + P:w + 2 * P], Kbd[:, c, :], ar, start=True, stop=True)
                    mm.then_inc(s["prod_done"], 1)
                for o in range(2):
                    fill(p + 1, o, EARLY)
                    after("rk_t", 2 * o + 1, 4)
                    each(AbT, lambda c: con(m, "ident"), 3 + 2 * o, o).then_inc(s["amat"], 1)
                fill(p + 1, 2, EARLY)
                for l in range(NL):
                    for o in range(2):
                        if l:
                            after("x", 2 * (l - 1) + o, 2 * (NL - 1))
                        else:
                            after("x1", o, 2)
                        each(AbT, lambda c: X[:, c, :], 3 + 2 * o, o).then_inc(s["tp"], 1)
                    fill(p + 2, 2 * l, share)
                    if l == 0:
                        after("xt1")
                    else:
                        after("xt", 2 * l - 1, 2 * NL)
                    for o in range(2):
                        after("t", 2 * l + o, 2 * NL)
                        if l < NL - 1:
                            each(XT, lambda c: TT[:, c, :], 3 + 2 * o, o)
                        each(TT, lambda c: XT[:, c, :], 4 + 2 * o, o).then_inc(s["xp"], 1)
                    fill(p + 2, 2 * l + 1, share)
                after("xt", 2 * NL - 1, 2 * NL)
                after("abd", 1, 2)
                for c in range(NCH):
                    if ahead:
                        prepare(p + 1, c)
                    if c:
                        after("s", c - 1, NCH)
                    w = pe.matmul(wcol, AkT[:, c, :], Vt[:, c, :], start=True, stop=c == 0)
                    if c:
                        w = pe.matmul(wcol, Abds[:, q, c, :], S[:, c % 2, :], start=False, stop=True)
                    w.then_inc(s["wp"], 1)
                    fill(p + 2, 10 + 3 * c, share)
                    after("w", c, NCH)
                    pe.matmul(ucol, XT[:, c, :], W[:], start=True, stop=True).then_inc(s["up"], 1)
                    fill(p + 2, 10 + 3 * c + 1, share)
                    after("u", c, NCH)
                    pe.matmul(scol, Kt[:, c, :], Vt[:, c, :], start=True, stop=False)
                    pe.matmul(scol, Bt[:, c, :], U[:], start=False, stop=True).then_inc(s["sp"], 1)
                    y = ybank[:, c * CH:(c + 1) * CH]
                    if c:
                        pe.matmul(y, S[:, c % 2, :], AR(q)[:, c, 1, :], start=True, stop=False)
                    pe.matmul(y, Vt[:, c, :], RkT[:, c, :], start=c == 0, stop=False)
                    pe.matmul(y, U[:], RbT[:, c, :], start=False, stop=True).then_inc(s["yp"], 1)
                    fill(p + 2, 10 + 3 * c + 2, share)
                after("y")
                pe.matmul(ybank[:], con(m, "heads"), row(z, p, 1), start=True, stop=True).then_inc(s["mean"], 1)
                fill(p + 2, 34, share)
                after("dev_sq")
                pe.matmul(ybank[:], con(m, "heads"), t1, start=True, stop=True).then_inc(s["var"], 1)
                fill(p + 2, 35, share)

            in_turn(pe, pair)


def stage_attention(nc, mem, m, d):
    NT = LATQ + LATKV + 1
    NS = 4
    NB, MOD0 = 4, 4
    MS = 2 * KD // NS
    names = ("squared", "sum", "root", "rstd", "lat", "tables", "swapped_k", "rot_k", "q_loaded", "k_loaded",
             "v_loaded", "proj", "copied", "swapped", "rot", "score", "max", "neg", "exp", "inv", "prob", "turned",
             "pt", "out", "y", "zeroed")
    with nc.cleanup_on_exit(), ExitStack() as ctx:
        s = {n: nc.alloc_semaphore("at_" + n) for n in names}
        s.update(mod_sems(nc, "at", NB))
        s.update(first_sems(nc, "at"))
        q, at = mem.put("at_q", [P, 4, T], F32, mem.h)
        k, at = mem.put("at_k", [P, 4, T], F32, at)
        v, at = mem.put("at_v", [P, 8, 2 * P], F32, at)
        qh, at = mem.put("at_qh", [P, 4, T], F32, at)
        rot, at = mem.put("at_rot", [P, 2, T], F32, at)
        pr, at = mem.put("at_p", [P, 4, T], F32, at)
        pt, at = mem.put("at_pt", [P, 4, T], F32, at)
        wq, at = mem.put("at_wq", [P, LATQ, 3 * P], F32, at)
        qr, at = mem.put("at_qr", [P, T], F32, at)
        lat, at = mem.put("at_lat", [P, NT, T], F32, mem.work)
        tables, at = mem.put("at_tables", [P, 2, T], F32, at)
        wk, at = mem.put("at_wk", [P, LATKV, 2 * P], F32, at)
        wv, at = mem.put("at_wv", [P, LATKV, 2 * P], F32, at)
        sq, at = mem.put("at_sq", [P, NT - 1, T], F32, at)
        rstd, at = mem.put("at_rstd", [P, 2, T], F32, at)
        nmax, at = mem.put("at_nmax", [P, 4], F32, at)
        den, at = mem.put("at_den", [P, 4], F32, at)
        mbuf, at = mem.put("at_mod_buf", [P, NB, GRP], F32, at)
        macc, at = mem.put("at_mod_acc", [P, 2, GRP], F32, at)
        cos, sin = tables[:, 0, :], tables[:, 1, :]
        kr = lat[:, NT - 1, :]
        bank, z = m["bank"], m["z"]
        raw = z[:, 8:8 + NT, :]
        groups = ((0, LATQ, "q_g"), (LATQ, LATKV, "kv_g"))
        HALF = (slice(0, CH), slice(CH, P))
        QR, SWAP_AFTER = 2, 4
        BANKS = {True: ((3, 4, 5, 6, 7, 1, 2), 0), False: ((7, 7, 7, 7, 3, 4, 5), 7)}
        ORDER = (3, 2, 0, 1)
        PLACE = {3: (0, 0), 2: (1, 0), 0: (1, 3 * P), 1: (2, 0)}
        LAST_OF_BANK = {3: 1, 2: 3, 0: 3, 1: 4}
        TURNED = {0: (3, 0), 1: (4, 0), 3: (4, -3 * P), 2: (5, -2 * P)}
        blk = ctx.enter_context(nc.Block())

        def scores(b):
            at, c0 = PLACE[b]
            return bank[at][:, c0:c0 + (b + 1) * P]

        def turned(c):
            at, c0 = TURNED[c]
            return bank[at][:, c0 + c * P:c0 + T]

        @blk.sync
        def _(sp):
            sp.dma_start(tables[:], d["tables"]).then_inc(s["tables"], 16)

            def load(i, tile, dram, name):
                w = tile.shape[2]
                sp.dma_start(tile[:], d[dram][i].rearrange("p (a n) -> p a n", n=w)).then_inc(s[name], 16)

            def load_step(i):
                if i:
                    sp.wait_ge(s["proj"], 7 * i - 4)
                load(i, wq, "w_q", "q_loaded")
                if i:
                    sp.wait_ge(s["proj"], 7 * i)
                load(i, wk, "w_k", "k_loaded")
                load(i, wv, "w_v", "v_loaded")

            load_step(0)
            for i in range(NS):
                if i + 1 < NS:
                    load_step(i + 1)
                if i == 0:
                    load_first(sp, m, s, d["w_out"])
                for j in range(MS):
                    u = i * MS + j
                    load_mod(sp, s, mbuf, u, u % NB, mod_unit(d, MOD0 * KD + u))

        @blk.gpsimd
        def _(pool):
            pool.memset(qh[:], 0.0).then_inc(s["zeroed"], 1)
            remainder_first(pool, m, s)

        @blk.tensor
        def _(pe):
            for t in range(NT - 1):
                pe.wait_ge(s["squared"], t + 1)
                n = t // LATQ
                mm = pe.matmul(bank[n][:], con(m, "ones"), sq[:, t, :], start=t in (0, LATQ),
                               stop=t in (LATQ - 1, NT - 2))
                if t in (LATQ - 1, NT - 2):
                    mm.then_inc(s["sum"], 1)
            pe.matmul(bank[2][:], con(m, "swap"), raw[:, NT - 1, :], start=True, stop=True)\
              .then_inc(s["swapped_k"], 1)

            def project(i, n):
                b = bank[BANKS[i == 0][0][n]]
                if n == 0:
                    pe.wait_ge(s["q_loaded"], 16 * (i + 1))
                if n == 3:
                    pe.wait_ge(s["k_loaded"], 16 * (i + 1))
                if n == 5:
                    pe.wait_ge(s["v_loaded"], 16 * (i + 1))
                if i == 0:
                    pe.wait_ge(s["lat"], LATQ if n < 3 else LATQ + LATKV)
                    if n == 6:
                        pe.wait_ge(s["rot_k"], 2)
                elif n in (1, 2, 3):
                    pe.wait_ge(s["copied"], 7 * i + n)
                elif n == 0 and i > 1:
                    pe.wait_ge(s["rot"], 4 * i - 2)
                if n < 3:
                    for c in range(LATQ):
                        mm = pe.matmul(b[:], wq[:, c, n * P:(n + 1) * P], lat[:, c, :], start=c == 0,
                                       stop=c == LATQ - 1)
                elif n < 5:
                    for c in range(LATKV):
                        mm = pe.matmul(b[:], wk[:, c, (n - 3) * P:(n - 2) * P], lat[:, LATQ + c, :], start=c == 0,
                                       stop=c == LATKV - 1)
                else:
                    for t in range(2):
                        rows = slice((2 * (n - 5) + t) * P, (2 * (n - 5) + t + 1) * P)
                        for c in range(LATKV):
                            mm = pe.matmul(b[:, t * 2 * P:(t + 1) * 2 * P], lat[:, LATQ + c, rows], wv[:, c, :],
                                           start=c == 0, stop=c == LATKV - 1)
                mm.then_inc(s["proj"], 1)
                if n == SWAP_AFTER:
                    pe.wait_ge(s["copied"], 7 * i + (QR + 1 if i == 0 else QR + 2))
                    pe.matmul(bank[BANKS[i == 0][1]][:], con(m, "swap"), qr[:], start=True, stop=True)\
                      .then_inc(s["swapped"], 1)

            for n in range(7):
                project(0, n)
            pe.wait_ge(s["rot_k"], 3)
            for i in range(NS):
                more = i + 1 < NS
                for h in range(2):
                    at = 2 * (i % 2) + h
                    n = 2 * i + h
                    if h == 0:
                        pe.wait_ge(s["copied"], 7 * (i + 1))
                        pe.wait_ge(s["rot"], 4 * (i + 1))
                    if n:
                        pe.wait_ge(s["exp"], 4 * n)
                    for b in ORDER:
                        w = (b + 1) * P
                        qs = slice(b * P, (b + 1) * P)
                        pe.matmul(scores(b), q[:, at, qs], k[:, at, 0:w], start=True, stop=False)
                        pe.matmul(scores(b), qh[:, at, qs], kr[:, 0:w], start=False, stop=False)
                        pe.matmul(scores(b)[:, b * P:w], con(m, "early"), con(m, "late"), start=False,
                                  stop=True).then_inc(s["score"], 1)
                    if more:
                        project(i + 1, 2 * h)
                    pe.wait_ge(s["prob"], 4 * n + 4)
                    for c in (0, 1, 3, 2):
                        for b in range(c, 4):
                            mm = pe.transpose(turned(c)[:, (b - c) * P:(b - c + 1) * P],
                                              pr[:, b, c * P:(c + 1) * P], con(m, "ident"))
                        mm.then_inc(s["turned"], 1)
                    if more:
                        project(i + 1, 2 * h + 1)
                    pe.wait_ge(s["pt"], 4 * n + 4)
                    if n:
                        pe.wait_ge(s["y"], n)
                    for c in range(4):
                        mm = pe.matmul(bank[6][:, c * P:T], v[:, 4 * (i % 2) + c, h * P:(h + 1) * P],
                                       pt[:, c, c * P:T], start=c == 0, stop=c == 3)
                    mm.then_inc(s["out"], 1)
                if more:
                    for piece in (4, 5, 6):
                        project(i + 1, piece)
            for g in range(2):
                mod_columns(pe, m, s, bank[0], macc[:, g, :], (MOD0 + g) * (GRP // P), KD * (g + 1) + NB)

        @blk.scalar
        def _(act):
            for t in range(NT - 1):
                act.activation(sq[:, t, :], raw[:, t, :], ACT.Square).then_inc(s["squared"], 1)
            for n, (t0, nt, _) in enumerate(groups):
                act.wait_ge(s["sum"], n + 1)
                act.activation(rstd[:, n, :], bank[n][:], ACT.Sqrt, bias=m["eps"][:, 0:1],
                               scale=1.0 / (nt * P)).then_inc(s["root"], 1)

            def copy(i, n):
                at = 2 * (i % 2)
                act.wait_ge(s["proj"], 7 * i + n + 1)
                if n < 2:
                    dst = q[:, at + n, :]
                elif n == 2:
                    dst = qr[:]
                elif n < 5:
                    dst = k[:, at + n - 3, :]
                else:
                    dst = v[:, 2 * at + 2 * (n - 5):2 * at + 2 * (n - 4), :].rearrange("p a n -> p (a n)")
                act.activation(dst, bank[BANKS[i == 0][0][n]][:], ACT.Copy).then_inc(s["copied"], 1)

            for n in range(7):
                copy(0, n)
            for i in range(NS):
                more = i + 1 < NS
                for h in range(2):
                    n = 2 * i + h
                    for b in ORDER:
                        act.wait_ge(s["neg"], 4 * n + LAST_OF_BANK[b])
                        act.activation(pr[:, b, 0:(b + 1) * P], scores(b), ACT.Exp, bias=nmax[:, b:b + 1],
                                       scale=SCALE, accum_out=den[:, b:b + 1]).then_inc(s["exp"], 1)
                    if more:
                        copy(i + 1, 2 * h)
                    for j, c in enumerate((0, 1, 3, 2)):
                        act.wait_ge(s["turned"], 4 * n + (1, 3, 3, 4)[j])
                        act.activation(pt[:, c, c * P:T], turned(c), ACT.Copy).then_inc(s["pt"], 1)
                    if more:
                        copy(i + 1, 2 * h + 1)
                    act.wait_ge(s["out"], n + 1)
                    if n == 0:
                        act.wait_ge(s["lat"], LATQ + LATKV)
                        act.wait_ge(s["rot_k"], 3)
                    act.activation(z[:, 8 + n, :], bank[6][:], ACT.Copy).then_inc(s["y"], 1)
                if more:
                    for piece in (4, 5, 6):
                        copy(i + 1, piece)
                if i == NS - 2:
                    round_first(act, m, s)

        @blk.vector
        def _(dve):
            dve.sem_inc(s["mod_summed"], NB)
            dve.sem_inc(s["mod_cols"], 2)
            for n, (t0, nt, g) in enumerate(groups):
                dve.wait_ge(s["root"], n + 1)
                dve.reciprocal(rstd[:, n, :], rstd[:, n, :]).then_inc(s["rstd"], 1)
                dve.wait_ge(s["rstd"], n + 1)
                for t in range(t0, t0 + nt):
                    dve.scalar_tensor_tensor(out=lat[:, t, :], in0=raw[:, t, :], scalar=vec(m, g, t - t0),
                                             in1=rstd[:, n, :], op0=ALU.mult, op1=ALU.mult).then_inc(s["lat"], 1)
            dve.wait_ge(s["tables"], 16)
            dve.wait_ge(s["swapped_k"], 1)
            dve.tensor_tensor(rot[:, 0, :], raw[:, NT - 1, :], cos, ALU.mult).then_inc(s["rot_k"], 1)
            dve.tensor_tensor(rot[:, 1, :], bank[2][:], sin, ALU.mult).then_inc(s["rot_k"], 1)
            dve.wait_ge(s["rot_k"], 2)
            dve.tensor_tensor(kr, rot[:, 0, :], rot[:, 1, :], ALU.add).then_inc(s["rot_k"], 1)
            dve.wait_ge(s["zeroed"], 1)
            dve.wait_ge(s["rot_k"], 3)

            def rotate(i):
                dve.wait_ge(s["copied"], 7 * i + QR + 1)
                dve.tensor_tensor(rot[:, 0, :], qr[:], cos, ALU.mult).then_inc(s["rot"], 1)
                dve.wait_ge(s["swapped"], i + 1)
                dve.tensor_tensor(rot[:, 1, :], bank[BANKS[i == 0][1]][:], sin, ALU.mult).then_inc(s["rot"], 1)
                dve.wait_ge(s["rot"], 4 * i + 2)
                for h in range(2):
                    dve.tensor_tensor(qh[HALF[h], 2 * (i % 2) + h, :], rot[HALF[h], 0, :], rot[HALF[h], 1, :],
                                      ALU.add).then_inc(s["rot"], 1)

            rotate(0)
            for i in range(NS):
                for h in range(2):
                    n = 2 * i + h
                    for j, b in enumerate(ORDER):
                        dve.wait_ge(s["score"], 4 * n + LAST_OF_BANK[b])
                        dve.tensor_reduce(nmax[:, b:b + 1], scores(b), AX_X, ALU.max).then_inc(s["max"], 1)
                        dve.wait_ge(s["max"], 4 * n + j + 1)
                        dve.tensor_scalar(nmax[:, b:b + 1], nmax[:, b:b + 1], -SCALE, None,
                                          ALU.mult).then_inc(s["neg"], 1)
                    for j, b in enumerate(ORDER):
                        w = (b + 1) * P
                        dve.wait_ge(s["exp"], 4 * n + j + 1)
                        dve.reciprocal(den[:, b:b + 1], den[:, b:b + 1]).then_inc(s["inv"], 1)
                        dve.wait_ge(s["inv"], 4 * n + j + 1)
                        dve.tensor_scalar(pr[:, b, 0:w], pr[:, b, 0:w], den[:, b:b + 1], None,
                                          ALU.mult).then_inc(s["prob"], 1)
                    for j in range(MS // 2):
                        u = i * MS + h * (MS // 2) + j
                        g, kt = u // KD, u % KD
                        add_mod(dve, m, s, mbuf, macc[:, g, :], u, u % NB, u // NB, NB, kt, kt == 0)
                if i + 1 < NS:
                    rotate(i + 1)
            finish_mod(dve, m, s, bank[0], 2 * KD, KD, 2, (2, "g_post_mix", 2 * KD))


def stage_mix_out(nc, mem, m, d):
    NB, MOD0, MG = 4, 6, 4
    MU = MG
    names = ("y_hi", "y_lo_pool", "y_lo_dve", "copied", "sq", "sq_added", "summed", "root", "rstd", "normed_dve",
             "normed_pool", "x_loaded", "x1_dve", "x1_pool")
    with nc.cleanup_on_exit(), ExitStack() as ctx:
        s = {n: nc.alloc_semaphore("mo_" + n) for n in names}
        s.update(ring_sems(nc, "mo"))
        s.update(mod_sems(nc, "mo", NB))
        o, at = mem.put("mo_o", [P, KD, T], F32, mem.work)
        sq, at = mem.put("mo_sq", [P, 2, T], F32, at)
        sq_sum, at = mem.put("mo_sq_sum", [P, T], F32, at)
        rstd, at = mem.put("mo_rstd", [P, T], F32, at)
        mbuf, at = mem.put("mo_mod_buf", [P, NB, GRP], F32, at)
        macc, at = mem.put("mo_mod_acc", [P, 2, GRP], F32, at)
        z, bank = m["z"], m["bank"]
        by_pool = [t for t in range(KD) if t % 8 in (2, 4, 6)]
        by_dve = [t for t in range(KD) if t not in by_pool]
        blk = ctx.enter_context(nc.Block())

        def wait_tile(eng, name, t):
            mine, who = (by_pool, "pool") if t in by_pool else (by_dve, "dve")
            eng.wait_ge(s[f"{name}_{who}"], mine.index(t) + 1)

        def residual(eng, mine, who):
            eng.wait_ge(s["rstd"], 1)
            eng.wait_ge(s["x_loaded"], 64)
            for n, t in enumerate(mine):
                eng.tensor_tensor(o[:, t, :], o[:, t, :], rstd[:], ALU.mult).then_inc(s["normed_" + who], 1)
                eng.wait_ge(s["normed_" + who], n + 1)
                eng.tensor_tensor(z[:, t, :], z[:, t, :], o[:, t, :], ALU.add).then_inc(s["x1_" + who], 1)

        def low(eng, who, t):
            eng.wait_ge(s["y_hi"], t + 1)
            eng.tensor_tensor(m["h_lo"][:, t, :], z[:, t, :], m["h_hi"][:, t, :].bitcast(F32),
                              ALU.subtract).then_inc(s["y_lo_" + who], 1)

        @blk.sync
        def _(sp):
            for j in range(2):
                load_unit(sp, m, s, 2 + j, j, 1, d["w_out"][2 + j], UNIT)
            sp.wait_ge(s["y_lo_pool"], KD // 2)
            sp.wait_ge(s["y_lo_dve"], KD // 2)

            def load_mods(t):
                for j in range(MU):
                    load_mod(sp, s, mbuf, t * MU + j, j % NB, mod_unit(d, t * MU + (MOD0 * KD + j)))

            for n in range(4):
                with sp.Fori(2 + 3 * n, 5 + 3 * n) as t:
                    for j in range(2):
                        load_unit(sp, m, s, t * 2 + j, j, t, row(d["w_out"], t * 2 + j), UNIT)
                    load_mods(t - 2)
                sp.dma_start(z[:, 4 * n:4 * n + 4, :], d["xt"][:, 4 * n:4 * n + 4, :]).then_inc(s["x_loaded"], 16)
            with sp.Fori(KD - 2, KD) as t:
                for j in range(2):
                    load_unit(sp, m, s, t * 2 + j, j, t, row(d["w_out"], t * 2 + j), UNIT)
                load_mods(t - 2)
            with sp.Fori(KD - 2, KD) as t:
                load_mods(t)

        @blk.gpsimd
        def _(pool):
            take_first(pool, s)
            for t in range(0, KD, 2):
                low(pool, "pool", t)
            pool.memset(sq_sum[:], 0.0).then_inc(s["sq_added"], 1)

            def tile(t, parity):
                for j in range(2):
                    remainder_unit(pool, m, s, t * 2 + j, j, UNIT)
                pool.wait_ge(s["sq"], t)
                pool.wait_ge(s["sq_added"], t)
                pool.tensor_tensor(sq_sum[:], sq_sum[:], sq[:, parity, :], ALU.add).then_inc(s["sq_added"], 1)

            with pool.Fori(0, KD // 2 - 1) as i:
                tile(i * 2 + 1, 0)
                tile(i * 2 + 2, 1)
            tile(KD - 1, 0)
            residual(pool, by_pool, "pool")

        @blk.scalar
        def _(act):
            for t in range(KD):
                act.activation(m["h_hi"][:, t, :], z[:, t, :], ACT.Copy).then_inc(s["y_hi"], 1)
            for t in range(KD):
                if t < KD - 1:
                    for j in range(2):
                        round_unit(act, m, s, 2 * t + 2 + j, j, t + 1, UNIT)
                tile_done(act, s, 2 * t + 1)
                if t >= 2:
                    act.wait_ge(s["sq_added"], t)
                act.activation(sq[:, t % 2, :], bank[t % 4][:], ACT.Square).then_inc(s["sq"], 1)
            act.wait_ge(s["summed"], 2)
            act.activation(rstd[:], bank[7][:], ACT.Sqrt, bias=m["eps"][:, 0:1], scale=1.0 / D).then_inc(s["root"], 1)
            for t in range(KD):
                wait_tile(act, "x1", t)
                if t >= 2:
                    act.wait_ge(s["summed"], 2 + t - 1)
                act.activation(sq[:, t % 2, :], z[:, t, :], ACT.Square).then_inc(s["sq"], 1)
            act.wait_ge(s["summed"], 2 + KD)
            act.activation(m["rstd"], bank[5][:], ACT.Sqrt, bias=m["eps"][:, 0:1], scale=1.0 / D)\
               .then_inc(s["root"], 1)

        @blk.vector
        def _(dve):
            dve.sem_inc(s["mod_summed"], NB)
            dve.sem_inc(s["mod_cols"], 2)
            for t in range(1, KD, 2):
                low(dve, "dve", t)
            with dve.Fori(0, 2) as i:
                for t in range(KD // 2):
                    for j in range(MU):
                        g, k = (t * MU + j) // KD, (t * MU + j) % KD
                        if k == 0:
                            dve.wait_ge(s["mod_cols"], i * 2 + (g + 1))
                        add_mod(dve, m, s, mbuf, macc[:, g, :], i * (2 * KD) + (t * MU + j), j, i * (KD // 2) + t,
                                NB, k, k == 0)
                    dve.wait_ge(s["sq"], i * (KD // 2) + (t + 1))
                    dve.tensor_scalar(row(o, i * (KD // 2) + t, 1), bank[t % 4][:],
                                      m["gs"][:, bass.ds(i * (KD // 2) + (2 * KD + t), 1)], None,
                                      ALU.mult).then_inc(s["copied"], 1)
            dve.wait_ge(s["root"], 1)
            dve.reciprocal(rstd[:], rstd[:]).then_inc(s["rstd"], 1)
            dve.wait_ge(s["copied"], KD)
            residual(dve, by_dve, "dve")
            finish_mod(dve, m, s, bank[6], MOD0 * (GRP // P), 2 * KD, MG, (1, "g_pre_ffn", 4 * KD))
            dve.wait_ge(s["root"], 2)
            dve.reciprocal(m["rstd"], m["rstd"])

        @blk.tensor
        def _(pe):
            pe.sem_inc(s["unit_used"], 2)
            for t in range(KD):
                if t >= 4:
                    pe.wait_ge(s["copied"], t - 3)
                for j in range(2):
                    if t == 0:
                        for k in range(0, 8, 2):
                            for who in ("pool", "dve"):
                                pe.wait_ge(s["y_lo_" + who], 4 * j + k // 2 + 1)
                            multiply_part(pe, m, s, j, j, bank[0][:], m["h_hi"], m["h_lo"], 8 * j, k, 2, 8,
                                          j == 0, j == 1)
                    else:
                        multiply_unit(pe, m, s, 2 * t + j, j, bank[t % 4][:], m["h_hi"], m["h_lo"], 8 * j, 8,
                                      j == 0, j == 1)
                if t % 4 == 1 and t > 1:
                    g = t // 4 - 1
                    mod_columns(pe, m, s, bank[6], macc[:, g % 2, :], (MOD0 + g) * (GRP // P), KD * (g + 1) + NB)
            pe.wait_ge(s["sq_added"], KD)
            pe.matmul(bank[7][:], con(m, "ones"), sq_sum[:], start=True, stop=False).then_inc(s["summed"], 1)
            pe.wait_ge(s["sq"], KD)
            pe.matmul(bank[7][:], con(m, "ones"), sq[:, (KD - 1) % 2, :], start=False, stop=True)\
              .then_inc(s["summed"], 1)
            mod_columns(pe, m, s, bank[6], macc[:, (MG - 1) % 2, :], (MOD0 + MG - 1) * (GRP // P), KD * MG + NB)
            for t in range(KD):
                pe.wait_ge(s["sq"], KD + t + 1)
                pe.matmul(bank[5][:], con(m, "ones"), sq[:, t % 2, :], start=t == 0, stop=t == KD - 1)\
                  .then_inc(s["summed"], 1)


def stage_ffn(nc, mem, m, d, out):
    names = ("gate_at", "gate_c1", "gate_c2", "gelu", "val_at", "val_c1", "val_c2", "hid", "hid_hi", "hid_lo",
             "share", "sq", "sq_added", "summed", "root", "rstd", "gained", "normed_dve", "normed_pool", "x2_dve",
             "x2_pool", "kept", "x1", "stored")
    UU = 4
    NB, MOD0 = 2, 10
    MW = T
    GU = GT * UU + KD
    with nc.cleanup_on_exit(), ExitStack() as ctx:
        s = {n: nc.alloc_semaphore("ff_" + n) for n in names}
        s.update(ring_sems(nc, "ff"))
        s.update(h_sems(nc, "ff"))
        s.update(mod_sems(nc, "ff", NB))
        acc = m["z"]
        at = put_ring(mem, m, "ff_w", DUNIT)
        h_hi, at = mem.put("ff_hid_hi", [P, GT, T], F32R, at)
        h_lo, at = mem.put("ff_hid_lo", [P, GT, T], F32R, at)
        gate, at = mem.put("ff_gate", [P, T], F32, at)
        val, at = mem.put("ff_val", [P, T], F32, at)
        hid, at = mem.put("ff_hid", [P, T], F32, at)
        rstd, at = mem.put("ff_rstd", [P, T], F32, at)
        sq_sum = rstd
        shared, at = mem.put("ff_shared", [P, NB + GROUPS, T], F32, at)
        mbuf, macc = shared[:, 0:NB, :], shared[:, NB:NB + GROUPS, :]
        tmp = shared[:, 0:4, :]
        x1, _ = mem.put("ff_x1", [P, KD, T], F32, mem.h)
        sq, _ = mem.put("ff_sq", [P, KD, T], F32, mem.h + KD * T * 4)
        by_pool = [t for t in range(KD) if t % 8 in (2, 4, 6)]
        by_dve = [t for t in range(KD) if t not in by_pool]
        bank = m["bank"]
        blk = ctx.enter_context(nc.Block())

        def residual(eng, mine, who):
            eng.wait_ge(s["rstd"], 1)
            eng.wait_ge(s["x1"], 16)
            for n, t in enumerate(mine):
                if who == "dve":
                    op = eng.scalar_tensor_tensor(out=acc[:, t, :], in0=acc[:, t, :],
                                                  scalar=m["gs"][:, 3 * KD + t:3 * KD + t + 1], in1=rstd[:],
                                                  op0=ALU.mult, op1=ALU.mult)
                else:
                    eng.wait_ge(s["gained"], n + 1)
                    op = eng.tensor_tensor(acc[:, t, :], acc[:, t, :], rstd[:], ALU.mult)
                op.then_inc(s["normed_" + who], 1)
                eng.wait_ge(s["normed_" + who], n + 1)
                eng.tensor_tensor(acc[:, t, :], x1[:, t, :], acc[:, t, :], ALU.add).then_inc(s["x2_" + who], 1)

        def conv(n, f):
            return vec(m, "conv", f + n * FT)

        @blk.sync
        def _(sp):
            def up(g):
                with sp.Fori(0, GT) as i:
                    for j in range(UU):
                        u = g * GU + i * UU + j
                        load_unit(sp, m, s, u, j % 2, g * (GU // 2) + i * 2 + (j // 2),
                                  row(d["w_up"], g * (GT * UU) + i * UU + j), UNIT)

            def down(g, first, last):
                with sp.Fori(first, last) as t:
                    for j in range(2):
                        u = g * GU + t * 2 + (GT * UU + j)
                        load_unit(sp, m, s, u, j, g * (GU // 2) + t + (GT * 2), row(d["w_down"], g * KD + t * 2 + j),
                                  DUNIT)
                        load_mod(sp, s, mbuf, g * KD + t * 2 + j, j, row(d["w_mod_gate"], g * KD + t * 2 + j))

            with sp.Fori(0, GROUPS - 1) as g:
                up(g)
                down(g, 0, KD // 2)
            up(GROUPS - 1)
            down(GROUPS - 1, 0, KD // 4)
            tile_done(sp, s, (GROUPS - 1) * GU + GT * UU - 1)
            sp.dma_start(x1[:], d["x1"]).then_inc(s["x1"], 16)
            down(GROUPS - 1, KD // 4, KD // 2)
            ends = (0, 4, 8, 12, 14, 16)
            for a, b in zip(ends, ends[1:]):
                for who, mine in (("dve", by_dve), ("pool", by_pool)):
                    sp.wait_ge(s["x2_" + who], sum(x < b for x in mine))
                sp.dma_start(out[:, a:b, :], acc[:, a:b, :]).then_inc(s["stored"], 16)
            sp.wait_ge(s["stored"], 16 * (len(ends) - 1))

        @blk.gpsimd
        def _(pool):
            pool.sem_inc(s["lo_ready"], 2)

            def tile(g, i, width):
                for j in range(2, 6):
                    remainder_unit(pool, m, s, g * GU + i * UU + j, j % 2, UNIT if j < 4 else width)
                pool.wait_ge(s["hid_hi"], g * GT + i + 1)
                pool.tensor_tensor(row(h_lo, i, 1), hid[:], row(h_hi, i, 1).bitcast(F32),
                                   ALU.subtract).then_inc(s["hid_lo"], 1)

            h_on_pool(pool, m, s, tmp, {2: lambda: remainder_unit(pool, m, s, 0, 0, UNIT),
                                        6: lambda: remainder_unit(pool, m, s, 1, 1, UNIT)})
            def group(g, last):
                with pool.Fori(0, GT - 1) as i:
                    tile(g, i, UNIT)
                tile(g, GT - 1, DUNIT)
                with pool.Fori(1, KD // 2) as t:
                    for j in range(2):
                        remainder_unit(pool, m, s, g * GU + t * 2 + (GT * UU + j), j, DUNIT)
                        if last:
                            pool.wait_ge(s["sq"], t * 2 + (j - 1))
                            pool.wait_ge(s["sq_added"], t * 2 + (j - 1))
                            pool.tensor_tensor(sq_sum[:], sq_sum[:], row(sq, t * 2 + (j - 2), 1),
                                               ALU.add).then_inc(s["sq_added"], 1)
                if not last:
                    for j in range(2):
                        remainder_unit(pool, m, s, g * GU + (GU + j), j, UNIT)

            with pool.Fori(0, GROUPS - 1) as g:
                group(g, False)
            pool.memset(sq_sum[:], 0.0).then_inc(s["sq_added"], 1)
            group(GROUPS - 1, True)
            residual(pool, by_pool, "pool")

        @blk.scalar
        def _(act):
            act.sem_inc(s["gelu"], 1)

            def square(t):
                act.wait_ge(s["share"], t + ((GROUPS - 1) * KD + 3))
                act.activation(row(sq, t, 1), row(acc, t, 1), ACT.Square).then_inc(s["sq"], 1)

            def tile(g, i, width):
                n = g * GT + i
                for j in (2, 3):
                    round_unit(act, m, s, g * GU + i * UU + j, j % 2, g * (GU // 2) + i * 2 + 1, UNIT)
                tile_done(act, s, g * GU + i * UU + 1)
                act.activation(gate[:], bank[0][:], ACT.Identity, scale=conv(2, n), bias=conv(3, n))\
                   .then_inc(s["gate_at"], 1)
                act.wait_ge(s["gate_c2"], n + 2)
                act.activation(gate[:], gate[:], ACT.Gelu_apprx_tanh).then_inc(s["gelu"], 1)
                for j in (4, 5):
                    round_unit(act, m, s, g * GU + i * UU + j, j % 2, g * (GU // 2) + i * 2 + 2, width)
                tile_done(act, s, g * GU + i * UU + 3)
                act.activation(val[:], bank[1][:], ACT.Identity, scale=conv(6, n), bias=conv(7, n))\
                   .then_inc(s["val_at"], 1)
                act.wait_ge(s["hid"], n + 1)
                act.activation(row(h_hi, i, 1), hid[:], ACT.Copy).then_inc(s["hid_hi"], 1)

            def group(g, last):
                with act.Fori(0, GT - 1) as i:
                    tile(g, i, UNIT)
                tile(g, GT - 1, DUNIT)
                with act.Fori(1, KD // 2) as t:
                    for j in range(2):
                        round_unit(act, m, s, g * GU + t * 2 + (GT * UU + j), j, g * (GU // 2) + t + (GT * 2), DUNIT)
                        if last:
                            square(t * 2 + (j - 2))
                if not last:
                    for j in range(2):
                        round_unit(act, m, s, g * GU + (GU + j), j, g * (GU // 2) + (GU // 2), UNIT)

            h_on_act(act, m, s, tmp, 3 * KD, {2: lambda: round_unit(act, m, s, 0, 0, 0, UNIT),
                                              6: lambda: round_unit(act, m, s, 1, 1, 0, UNIT),
                                              8: lambda: act.dma_start(d["x1"], acc[:]).then_inc(s["kept"], 16)})
            with act.Fori(0, GROUPS - 1) as g:
                group(g, False)
            group(GROUPS - 1, True)
            for t in range(KD - 2, KD):
                square(t)
            act.wait_ge(s["summed"], 3)
            act.activation(rstd[:], bank[7][:], ACT.Sqrt, bias=m["eps"][:, 0:1], scale=1.0 / D).then_inc(s["root"], 1)
            act.wait_ge(s["mod_added"], 2)
            for t in by_pool:
                act.activation(acc[:, t, :], acc[:, t, :], ACT.Copy,
                               scale=m["gs"][:, 3 * KD + t:3 * KD + t + 1]).then_inc(s["gained"], 1)

        @blk.vector
        def _(dve):
            h_on_dve(dve, m, s, tmp, 1, 3 * KD)
            wait_h(dve, s, KD - 1)
            dve.wait_ge(s["kept"], 16)
            dve.memset(acc[:], 0.0).then_inc(s["share"], 1)
            dve.sem_inc(s["share"], 1)
            dve.sem_inc(s["mod_summed"], NB - 1)
            dve.sem_inc(s["mod_cols"], 2)
            dve.memset(macc[:], 0.0).then_inc(s["mod_summed"], 1)
            with dve.Fori(0, GROUPS) as g:
                with dve.Fori(0, GT) as i:
                    n = g * GT + i
                    for tile, b, at, c1, c2, w in ((gate, 0, "gate_at", "gate_c1", "gate_c2", 0),
                                                   (val, 1, "val_at", "val_c1", "val_c2", 4)):
                        dve.wait_ge(s[at], n + 1)
                        dve.scalar_tensor_tensor(out=tile[:, 1:T], in0=bank[b][:, 0:T - 1], scalar=conv(w + 1, n),
                                                 in1=tile[:, 1:T], op0=ALU.mult, op1=ALU.add).then_inc(s[c1], 1)
                        dve.wait_ge(s[c1], n + 1)
                        dve.scalar_tensor_tensor(out=tile[:, 2:T], in0=bank[b][:, 0:T - 2], scalar=conv(w, n),
                                                 in1=tile[:, 2:T], op0=ALU.mult, op1=ALU.add).then_inc(s[c2], 1)
                    dve.wait_ge(s["val_c2"], n + 2)
                    dve.wait_ge(s["gelu"], n + 2)
                    dve.wait_ge(s["hid_lo"], n + 1)
                    dve.tensor_tensor(hid[:], gate[:], val[:], ALU.mult).then_inc(s["hid"], 1)
                with dve.Fori(0, KD // 2) as t:
                    for j in range(2):
                        add_mod(dve, m, s, mbuf, row(macc, g, 1), g * KD + t * 2 + j, j, g * (KD // 2) + t, NB,
                                t * 2 + j)
                        tile_done(dve, s, g * GU + t * 2 + (GT * UU + j))
                        dve.wait_ge(s["share"], g * KD + t * 2 + (j + 2))
                        o = row(acc, t * 2 + j, 1)
                        dve.tensor_tensor(o, bank[2 + j][:], o, ALU.add).then_inc(s["share"], 1)
            finish_mod(dve, m, s, bank[4], 5 * KD, KD, GROUPS, (3, "g_post_ffn", 5 * KD))
            dve.wait_ge(s["root"], 1)
            dve.reciprocal(rstd[:], rstd[:]).then_inc(s["rstd"], 1)
            residual(dve, by_dve, "dve")

        @blk.tensor
        def _(pe):
            pe.sem_inc(s["unit_used"], 2)
            pe.sem_inc(s["gate_c2"], 1)
            pe.sem_inc(s["val_c2"], 1)
            pe.sem_inc(s["hid_lo"], 1)
            with pe.Fori(0, GROUPS) as g:
                with pe.Fori(0, GT) as i:
                    n = g * GT + i
                    for b in range(2):
                        pe.wait_ge(s[("gate_c2", "val_c2")[b]], n + 1)
                        for j in (2 * b, 2 * b + 1):
                            if j < 2:
                                multiply_first(pe, m, s, g * GU + i * UU + j, j, bank[0][:], 8 * j, j == 0, j == 1)
                                continue
                            multiply_unit(pe, m, s, g * GU + i * UU + j, j % 2, bank[b][:], m["h_hi"], m["h_lo"],
                                          8 * (j % 2), 8, j % 2 == 0, j % 2 == 1)
                with pe.Fori(0, KD // 2) as t:
                    for j in range(2):
                        pe.wait_ge(s["share"], g * KD + t * 2 + (j + 1))
                        for at, n in ((0, GT - 1), (GT - 1, 1)):
                            if j == 0:
                                pe.wait_ge(s["hid_lo"], g * GT + (at + n + 1))
                            multiply_part(pe, m, s, g * GU + t * 2 + (GT * UU + j), j, bank[2 + j][:], h_hi, h_lo,
                                          0, at, n, GT, True, True)
            pe.wait_ge(s["sq_added"], KD - 1)
            pe.matmul(bank[7][:], con(m, "ones"), sq_sum[:], start=True, stop=False).then_inc(s["summed"], 1)
            for t in range(KD - 2, KD):
                pe.wait_ge(s["sq"], t + 1)
                pe.matmul(bank[7][:], con(m, "ones"), sq[:, t, :], start=False, stop=t == KD - 1)\
                  .then_inc(s["summed"], 1)
                if t == KD - 2:
                    for g in range(GROUPS):
                        mod_columns(pe, m, s, bank[4], macc[:, g, :], 5 * KD + g * (MW // P), GROUPS * KD + NB)


def kernel(**inputs):
    from concourse import bacc
    from concourse.bass_utils import run_bass_kernel_spmd

    a = {n: np.asarray(v) for n, v in inputs.items()}

    def cols(v):
        return np.ascontiguousarray(v.reshape(-1, P).T)

    def zeros(rows, width):
        return np.zeros((rows, width), np.float32)

    def units(w, kt):
        K, M = w.shape
        v = w.reshape(K // (kt * P), kt, P, M // P, P)
        return np.ascontiguousarray(v.transpose(3, 0, 2, 1, 4)).reshape(-1, P, kt * P)

    w = a["w_in"][0]
    lo = [3072, 3168, 3264, 3520, 4032, 4288, 4352]
    mu = a["mu_shift"][0]
    pad = zeros(D, 32)
    parts = [w[:, lo[2]:lo[3]], w[:, lo[0]:lo[1]], pad, w[:, lo[1]:lo[2]], pad]
    for p in range(NPAIR):
        parts += [w[:, g * 1024 + p * P:g * 1024 + (p + 1) * P] for g in range(3)]
    parts += [w[:, lo[3]:lo[5]], w[:, lo[5]:], w[:, lo[5]:]]
    w_in = units(np.concatenate(parts, 1), 8)
    z32 = np.zeros(32, np.float32)
    mu_cols = np.concatenate([mu[:3072], mu[lo[2]:lo[3]], mu[lo[0]:lo[1]], z32, mu[lo[1]:lo[2]], z32])
    cw, cb = a["conv_w"][0], a["conv_b"][0]
    conv = np.concatenate([np.concatenate([cw[0, h], cw[1, h], cw[2, h], cb[h]])
                           for h in (slice(0, FF), slice(FF, 2 * FF))])
    parts = [a["c"][0], a["b_mod"][0], a["g_pre_mix"][0], a["g_post_mix"][0], a["g_pre_ffn"][0], a["g_post_ffn"][0],
             mu_cols, a["w0"][0], a["a0"][0], a["k_k"][0], a["k_a"][0], a["r_k"][0].reshape(-1), a["ln_x_g"][0],
             a["ln_x_b"][0], a["q_norm_g"][0], a["kv_norm_g"][0], conv]
    vecs = cols(np.concatenate(parts))
    low = np.concatenate([a["w_gate_up"][0], a["w_decay_up"][0], zeros(32, 1024), a["w_iclr_up"][0], zeros(32, 1024)])
    low = np.ascontiguousarray(low.reshape(4, P, NPAIR, P).transpose(2, 1, 0, 3)).reshape(NPAIR, P, 4 * P)
    wq = a["w_q_up"][0].reshape(LATQ, P, 4, 2, NOPE + ROPE)
    wq = np.concatenate([wq[..., 0, :NOPE], wq[..., 1, :NOPE], wq[..., 0, NOPE:], wq[..., 1, NOPE:]], -1)
    wq = np.ascontiguousarray(wq.transpose(2, 1, 0, 3)).reshape(4, P, LATQ * 3 * P)
    wkv = a["w_kv_up"][0].reshape(LATKV, P, 4, 2, 2, P)
    wk, wv = (np.ascontiguousarray(wkv[:, :, :, :, n].transpose(2, 1, 0, 3, 4)).reshape(4, P, LATKV * 2 * P)
              for n in range(2))
    wm = a["w_mod"][0][:, :5 * D].reshape(KD, P, 5 * D // GRP, GRP)
    wm = np.ascontiguousarray(wm.transpose(2, 0, 1, 3)).reshape(-1, P, GRP)
    wg = a["w_mod"][0][:, 5 * D:].reshape(KD, P, GROUPS, D // GROUPS)
    wg = np.ascontiguousarray(wg.transpose(2, 0, 1, 3)).reshape(-1, P, D // GROUPS)
    up = a["w_ffn_up"][0].reshape(2, 8, P, 2, FT, P)
    up = np.ascontiguousarray(up.transpose(4, 3, 0, 2, 1, 5)).reshape(FT * 4, P, UNIT)
    dn = a["w_ffn_down"][0].reshape(GROUPS, GT, P, KD, P)
    dn = np.ascontiguousarray(dn.transpose(0, 3, 2, 1, 4)).reshape(GROUPS * KD, P, DUNIT)
    xt = np.ascontiguousarray(a["x"][0].T.reshape(KD, P, T).transpose(1, 0, 2))
    pos = np.ascontiguousarray(np.broadcast_to(a["positions"][0][None, :], (P, T)))

    arrays = {"vec": vecs, "con": constants(), "xt": xt, "pos": pos, "w_mod": wm, "w_mod_gate": wg,
              "w_in": w_in, "low": low,
              "w_q": wq, "w_k": wk, "w_v": wv, "w_out": units(a["w_out"][0], 8), "w_up": up, "w_down": dn}
    nc = bacc.Bacc("TRN2", target_bir_lowering=False, num_devices=1)
    d = {n: nc.dram_tensor("in_" + n, v.shape, mybir.dt.from_np(v.dtype), kind="ExternalInput").ap()
         for n, v in arrays.items()}
    d["tables"] = nc.dram_tensor("rotary_tables", (P, 2, T), F32, kind="Internal").ap()
    d["x1"] = nc.dram_tensor("x1_kept", (P, KD, T), F32, kind="Internal").ap()
    out = nc.dram_tensor("out", (P, KD, T), F32, kind="ExternalOutput").ap()
    build_program(nc, d, out)
    r = run_bass_kernel_spmd(nc, [{"in_" + n: v for n, v in arrays.items()}], core_ids=[0])
    got = r.results[0]["out"]
    return np.ascontiguousarray(got.transpose(1, 0, 2).reshape(D, T).T).reshape(1, T, D)
```
